# Optimizing a Trainium2 kernel written in Bass

```python
import jax, jax.numpy as jnp
from jax import lax
import numpy as np

D_MODEL = 2048
BATCH = 1
SEQ = 256
DEPTH = 1

CTX_LEN = 256
GRID_W = 64
MIX_W = D_MODEL
HEAD_SIZE = 128
ATTN_W = MIX_W // 2
N_HEADS = ATTN_W // HEAD_SIZE
QK_NOPE = 128
QK_ROPE = 64
V_DIM = HEAD_SIZE
Q_RANK = D_MODEL // 4
KV_RANK = D_MODEL // 8
CONV_W = MIX_W - ATTN_W
CONV_GROUPS = CONV_W // HEAD_SIZE
N_GROUPS = MIX_W // HEAD_SIZE
FFN_DIM = ((8 * D_MODEL // 3 + 127) // 128) * 128
IN_COLS = Q_RANK + KV_RANK + QK_ROPE + 3 * CONV_W
ROPE_BASE = 10000.0
Q_BLOCK = 128
EPS = 1e-6


def rms_norm(x, g):
    xf = x.astype(jnp.float32)
    y = xf * lax.rsqrt(jnp.mean(xf * xf, axis=-1, keepdims=True) + EPS)
    return (y * g.astype(jnp.float32)).astype(x.dtype)

def modulate(h, shift, scale):
    return h * (1 + scale) + shift

def axial_rope_tables(n_tok, dtype):
    rows = n_tok // GRID_W
    row = jnp.repeat(jnp.arange(rows), GRID_W).astype(jnp.float32)
    col = jnp.tile(jnp.arange(GRID_W), rows).astype(jnp.float32)
    axis_dim = QK_ROPE // 2
    inv = ROPE_BASE ** (-jnp.arange(0, axis_dim, 2, dtype=jnp.float32) / axis_dim)
    ang = jnp.concatenate([row[:, None] * inv, col[:, None] * inv], axis=-1)
    return jnp.cos(ang).astype(dtype), jnp.sin(ang).astype(dtype)

def apply_rope(x, cos, sin):
    xp = x.reshape(*x.shape[:-1], QK_ROPE // 2, 2)
    x1, x2 = xp[..., 0], xp[..., 1]
    return jnp.stack([x1 * cos - x2 * sin, x1 * sin + x2 * cos], axis=-1).reshape(x.shape)

def dwconv3(x, w, b):
    xp = jnp.pad(x, ((0, 0), (1, 1), (0, 0)))
    return xp[:, :-2] * w[0] + xp[:, 1:-1] * w[1] + xp[:, 2:] * w[2] + b

def split_projection(p):
    cuts = [Q_RANK, Q_RANK + KV_RANK, Q_RANK + KV_RANK + QK_ROPE,
            Q_RANK + KV_RANK + QK_ROPE + CONV_W, Q_RANK + KV_RANK + QK_ROPE + 2 * CONV_W]
    return jnp.split(p, cuts, axis=-1)

def mla_query(q_a, g_q_a, w_q_b, rope):
    b, l, _ = q_a.shape
    q = (rms_norm(q_a, g_q_a) @ w_q_b).reshape(b, l, N_HEADS, QK_NOPE + QK_ROPE).transpose(0, 2, 1, 3)
    q_nope, q_rope = q[..., :QK_NOPE], q[..., QK_NOPE:]
    if rope is not None:
        q_rope = apply_rope(q_rope, *rope)
    return jnp.concatenate([q_nope, q_rope], axis=-1)

def mla_key_value(kv_a, k_rope, g_kv_a, w_kv_b, rope):
    b, l, _ = kv_a.shape
    kv = (rms_norm(kv_a, g_kv_a) @ w_kv_b).reshape(b, l, N_HEADS, QK_NOPE + V_DIM).transpose(0, 2, 1, 3)
    k_nope, v = kv[..., :QK_NOPE], kv[..., QK_NOPE:]
    if rope is not None:
        k_rope = apply_rope(k_rope, *rope)
    k_rope = jnp.broadcast_to(k_rope[:, None], (b, N_HEADS, l, QK_ROPE))
    return jnp.concatenate([k_nope, k_rope], axis=-1), v

def block_attention(q, k, v):
    b, h, l, dqk = q.shape
    nb = l // Q_BLOCK
    scale = (QK_NOPE + QK_ROPE) ** -0.5
    qb = q.reshape(b, h, nb, Q_BLOCK, dqk).transpose(2, 0, 1, 3, 4)

    def one_block(qi):
        s = jnp.einsum("bhqd,bhkd->bhqk", qi, k).astype(jnp.float32) * scale
        p = jax.nn.softmax(s, axis=-1).astype(v.dtype)
        return jnp.einsum("bhqk,bhkd->bhqd", p, v)

    o = lax.map(one_block, qb)
    return o.transpose(1, 0, 3, 2, 4).reshape(b, l, h * V_DIM)

def short_conv(gate_b, gate_c, hc, w, bias):
    return gate_b * dwconv3(gate_c * hc, w, bias)

def merge_heads(att, conv, g_mix, w_out):
    b, l, _ = att.shape
    mix = jnp.concatenate([att, conv], axis=-1).reshape(b, l, N_GROUPS, HEAD_SIZE)
    mix = rms_norm(mix, g_mix.reshape(N_GROUPS, HEAD_SIZE)).reshape(b, l, MIX_W)
    return mix @ w_out

def conv_ffn(h, w_up, cw, cb, w_down):
    u = dwconv3(h @ w_up, cw, cb)
    a, g = jnp.split(u, 2, axis=-1)
    return (a * jax.nn.silu(g)) @ w_down

def first_inputs(seed: int = 0) -> dict:
    key = jax.random.key(seed)
    ks = jax.random.split(key, 24)
    f32 = jnp.float32
    nrm = lambda k, shape, s: jax.random.normal(k, shape, f32) * s
    gain = lambda k, shape: 1.0 + 0.02 * jax.random.normal(k, shape, f32)
    return {
        "x": nrm(ks[0], (BATCH, SEQ, D_MODEL), 1.0),
        "c": nrm(ks[1], (BATCH, D_MODEL), 1.0),
        "ctx": nrm(ks[2], (BATCH, CTX_LEN, D_MODEL), 1.0),
        "c_ctx": nrm(ks[3], (D_MODEL,), 1.0),
        "w_ada": nrm(ks[4], (DEPTH, D_MODEL, 6 * D_MODEL), D_MODEL ** -0.5),
        "b_ada": nrm(ks[5], (DEPTH, 6 * D_MODEL), 0.01),
        "g_mix_norm": gain(ks[6], (DEPTH, D_MODEL)),
        "w_in": nrm(ks[7], (DEPTH, D_MODEL, IN_COLS), D_MODEL ** -0.5),
        "g_q_a": gain(ks[8], (DEPTH, Q_RANK)),
        "w_q_b": nrm(ks[9], (DEPTH, Q_RANK, N_HEADS * (QK_NOPE + QK_ROPE)), Q_RANK ** -0.5),
        "g_kv_a": gain(ks[10], (DEPTH, KV_RANK)),
        "w_kv_b": nrm(ks[11], (DEPTH, KV_RANK, N_HEADS * (QK_NOPE + V_DIM)), KV_RANK ** -0.5),
        "conv_w": nrm(ks[12], (DEPTH, 3, CONV_W), 3 ** -0.5),
        "conv_b": nrm(ks[13], (DEPTH, CONV_W), 0.01),
        "g_mix_out": gain(ks[14], (DEPTH, MIX_W)),
        "w_out": nrm(ks[15], (DEPTH, MIX_W, D_MODEL), MIX_W ** -0.5),
        "g_ffn_norm": gain(ks[16], (DEPTH, D_MODEL)),
        "w_up": nrm(ks[17], (DEPTH, D_MODEL, 2 * FFN_DIM), D_MODEL ** -0.5),
        "ffn_conv_w": nrm(ks[18], (DEPTH, 3, 2 * FFN_DIM), 3 ** -0.5),
        "ffn_conv_b": nrm(ks[19], (DEPTH, 2 * FFN_DIM), 0.01),
        "w_down": nrm(ks[20], (DEPTH, FFN_DIM, D_MODEL), FFN_DIM ** -0.5),
        "g_final": gain(ks[21], (D_MODEL,)),
    }

def first_block(x, c, ctx, c_ctx, w_ada, b_ada, g_mix_norm, w_in, g_q_a, w_q_b, g_kv_a, w_kv_b,
              conv_w, conv_b, g_mix_out, w_out, g_ffn_norm, w_up, ffn_conv_w, ffn_conv_b,
              w_down, g_final):
    n_tok = x.shape[1]
    rope_lat = axial_rope_tables(n_tok, x.dtype)
    xc = ctx
    for l in range(DEPTH):
        last = l == DEPTH - 1
        mod_l = (jax.nn.silu(c) @ w_ada[l] + b_ada[l])[:, None, :]
        mod_c = (jax.nn.silu(c_ctx) @ w_ada[l] + b_ada[l])[None, None, :]
        sh_a, sc_a, gt_a, sh_f, sc_f, gt_f = jnp.split(mod_l, 6, axis=-1)
        csh_a, csc_a, cgt_a, csh_f, csc_f, cgt_f = jnp.split(mod_c, 6, axis=-1)

        h_l = modulate(rms_norm(x, g_mix_norm[l]), sh_a, sc_a)
        h_c = modulate(rms_norm(xc, g_mix_norm[l]), csh_a, csc_a)
        qa_l, kva_l, kr_l, cb_l, cc_l, ch_l = split_projection(h_l @ w_in[l])
        qa_c, kva_c, kr_c, cb_c, cc_c, ch_c = split_projection(h_c @ w_in[l])

        k_l, v_l = mla_key_value(kva_l, kr_l, g_kv_a[l], w_kv_b[l], rope_lat)
        k_c, v_c = mla_key_value(kva_c, kr_c, g_kv_a[l], w_kv_b[l], None)
        q_l = mla_query(qa_l, g_q_a[l], w_q_b[l], rope_lat)
        att_l = block_attention(q_l, jnp.concatenate([k_l, k_c], axis=2),
                                jnp.concatenate([v_l, v_c], axis=2))
        conv_l = short_conv(cb_l, cc_l, ch_l, conv_w[l], conv_b[l])
        x = x + gt_a * merge_heads(att_l, conv_l, g_mix_out[l], w_out[l])

        if not last:
            q_c = mla_query(qa_c, g_q_a[l], w_q_b[l], None)
            att_c = block_attention(q_c, k_c, v_c)
            conv_c = short_conv(cb_c, cc_c, ch_c, conv_w[l], conv_b[l])
            xc = xc + cgt_a * merge_heads(att_c, conv_c, g_mix_out[l], w_out[l])
            hf_c = modulate(rms_norm(xc, g_ffn_norm[l]), csh_f, csc_f)
            xc = xc + cgt_f * conv_ffn(hf_c, w_up[l], ffn_conv_w[l], ffn_conv_b[l], w_down[l])

        hf_l = modulate(rms_norm(x, g_ffn_norm[l]), sh_f, sc_f)
        x = x + gt_f * conv_ffn(hf_l, w_up[l], ffn_conv_w[l], ffn_conv_b[l], w_down[l])
    return rms_norm(x, g_final)


HEAD_DIM = 128
N_HEADS_MOBA = D_MODEL // (2 * HEAD_DIM)
N_HEADS_FOX = D_MODEL // (2 * HEAD_DIM)
MOBA_WIDTH = N_HEADS_MOBA * HEAD_DIM
FOX_WIDTH = N_HEADS_FOX * HEAD_DIM
MOBA_BLOCK = 256
MOBA_TOPK = 3
MOBA_Q_CHUNK = 64
FOX_Q_BLOCK = 128
D_FF = 4 * D_MODEL
RMS_EPS = 1e-6
IN_WIDTHS = (MOBA_WIDTH, MOBA_WIDTH, MOBA_WIDTH,
             FOX_WIDTH, FOX_WIDTH, FOX_WIDTH,
             N_HEADS_FOX,
             D_MODEL, D_MODEL)
D_IN = sum(IN_WIDTHS)


def rms_norm_2(x, g):
    xf = x.astype(jnp.float32)
    y = xf * lax.rsqrt(jnp.mean(xf * xf, axis=-1, keepdims=True) + RMS_EPS)
    return (y * g.astype(jnp.float32)).astype(x.dtype)

def split_heads(t, n_heads):
    b, s, _ = t.shape
    return t.reshape(b, s, n_heads, HEAD_DIM).transpose(0, 2, 1, 3)

def merge_heads_2(t):
    b, h, s, d = t.shape
    return t.transpose(0, 2, 1, 3).reshape(b, s, h * d)

def to_chunks(a, c):
    a = a.reshape(a.shape[:2] + (a.shape[2] // c, c) + a.shape[3:])
    return jnp.moveaxis(a, 2, 0)

def from_chunks(a):
    a = jnp.moveaxis(a, 0, 2)
    return a.reshape(a.shape[:2] + (a.shape[2] * a.shape[3],) + a.shape[4:])

def alibi_slopes(n_heads):
    return jnp.exp2(-8.0 * jnp.arange(1, n_heads + 1, dtype=jnp.float32) / n_heads)

def moba_attention(q, k, v):
    b, h, s, d = q.shape
    s_pad = -(-s // MOBA_BLOCK) * MOBA_BLOCK
    pad = ((0, 0), (0, 0), (0, s_pad - s), (0, 0))
    q, k, v = jnp.pad(q, pad), jnp.pad(k, pad), jnp.pad(v, pad)
    nb = s_pad // MOBA_BLOCK
    n_sel = min(MOBA_TOPK, nb)
    scale = HEAD_DIM ** -0.5
    slopes = alibi_slopes(h)[None, :, None]
    kb = k.reshape(b, h, nb, MOBA_BLOCK, d)
    vb = v.reshape(b, h, nb, MOBA_BLOCK, d)
    kmean = jnp.mean(kb.astype(jnp.float32), axis=3)
    gate = jnp.einsum('bhtd,bhnd->bhtn', q.astype(jnp.float32), kmean)
    q_blk = jnp.arange(s_pad) // MOBA_BLOCK
    past = jnp.arange(nb)[None, :] < q_blk[:, None]
    gate = jnp.where(past, gate, -jnp.inf)
    top_vals, sel = lax.top_k(gate, n_sel)
    valid = jnp.isfinite(top_vals)
    bi = jnp.arange(b)[:, None, None, None]
    hi = jnp.arange(h)[None, :, None, None]
    blk_off = jnp.arange(MOBA_BLOCK)

    def chunk(args):
        ci, qc, selc, validc = args
        q_pos = ci * MOBA_Q_CHUNK + jnp.arange(MOBA_Q_CHUNK)
        own = (ci * MOBA_Q_CHUNK) // MOBA_BLOCK
        k_own = lax.dynamic_index_in_dim(kb, own, axis=2, keepdims=False)
        v_own = lax.dynamic_index_in_dim(vb, own, axis=2, keepdims=False)
        dist_own = (q_pos[:, None] - (own * MOBA_BLOCK + blk_off)[None, :])
        s_own = jnp.einsum('bhcd,bhsd->bhcs', qc, k_own).astype(jnp.float32) * scale
        s_own = s_own - slopes[..., None] * jnp.abs(dist_own).astype(jnp.float32)
        s_own = jnp.where(dist_own >= 0, s_own, -jnp.inf)
        k_sel = kb[bi, hi, selc]
        v_sel = vb[bi, hi, selc]
        s_sel = jnp.einsum('bhcd,bhcjsd->bhcjs', qc, k_sel).astype(jnp.float32) * scale
        sel_pos = selc[..., None] * MOBA_BLOCK + blk_off
        dist_sel = jnp.abs(q_pos[None, None, :, None, None] - sel_pos).astype(jnp.float32)
        s_sel = s_sel - slopes[..., None, None] * dist_sel
        s_sel = jnp.where(validc[..., None], s_sel, -jnp.inf)
        c, j = selc.shape[2], selc.shape[3]
        scores = jnp.concatenate([s_sel.reshape(b, h, c, j * MOBA_BLOCK), s_own], axis=-1)
        p = jax.nn.softmax(scores, axis=-1).astype(v.dtype)
        p_sel = p[..., :j * MOBA_BLOCK].reshape(b, h, c, j, MOBA_BLOCK)
        p_own = p[..., j * MOBA_BLOCK:]
        return (jnp.einsum('bhcjs,bhcjsd->bhcd', p_sel, v_sel)
                + jnp.einsum('bhcs,bhsd->bhcd', p_own, v_own))

    nc = s_pad // MOBA_Q_CHUNK
    out = lax.map(chunk, (jnp.arange(nc), to_chunks(q, MOBA_Q_CHUNK),
                          to_chunks(sel, MOBA_Q_CHUNK), to_chunks(valid, MOBA_Q_CHUNK)))
    return from_chunks(out)[:, :, :s]

def forgetting_attention(q, k, v, f_logit, b_forget):
    b, h, s, d = q.shape
    scale = HEAD_DIM ** -0.5
    log_f = jax.nn.log_sigmoid(f_logit.astype(jnp.float32) + b_forget.astype(jnp.float32))
    c = jnp.cumsum(log_f, axis=1).transpose(0, 2, 1)
    key_pos = jnp.arange(s)

    def chunk(args):
        ci, qc, cq = args
        sc = jnp.einsum('bhcd,bhsd->bhcs', qc, k).astype(jnp.float32) * scale
        sc = sc + cq[..., None] - c[:, :, None, :]
        q_pos = ci * FOX_Q_BLOCK + jnp.arange(FOX_Q_BLOCK)
        sc = jnp.where(q_pos[:, None] >= key_pos[None, :], sc, -jnp.inf)
        p = jax.nn.softmax(sc, axis=-1).astype(v.dtype)
        return jnp.einsum('bhcs,bhsd->bhcd', p, v)

    nc = s // FOX_Q_BLOCK
    cq = c.reshape(b, h, nc, FOX_Q_BLOCK).transpose(2, 0, 1, 3)
    out = lax.map(chunk, (jnp.arange(nc), to_chunks(q, FOX_Q_BLOCK), cq))
    return from_chunks(out)

def second_inputs(seed: int = 0) -> dict:
    key = jax.random.key(seed)
    ks = jax.random.split(key, 11)
    f32 = jnp.float32
    def normal(k, shape, scale):
        return jax.random.normal(k, shape, f32) * scale
    return {
        "x": normal(ks[0], (BATCH, SEQ, D_MODEL), 1.0),
        "norm_mix_g": 1.0 + normal(ks[1], (D_MODEL,), 0.02),
        "w_in": normal(ks[2], (D_MODEL, D_IN), D_MODEL ** -0.5),
        "b_forget": 2.0 + normal(ks[3], (N_HEADS_FOX,), 0.5),
        "w_proj_a": normal(ks[4], (MOBA_WIDTH, D_MODEL), MOBA_WIDTH ** -0.5),
        "w_proj_b": normal(ks[5], (FOX_WIDTH, D_MODEL), FOX_WIDTH ** -0.5),
        "w_out": normal(ks[6], (D_MODEL, D_MODEL), D_MODEL ** -0.5),
        "norm_mlp_g": 1.0 + normal(ks[7], (D_MODEL,), 0.02),
        "w_up": normal(ks[8], (D_MODEL, D_FF), D_MODEL ** -0.5),
        "w_down": normal(ks[9], (D_FF, D_MODEL), D_FF ** -0.5),
        "norm_final_g": 1.0 + normal(ks[10], (D_MODEL,), 0.02),
    }

def second_block(x, norm_mix_g, w_in, b_forget, w_proj_a, w_proj_b, w_out,
              norm_mlp_g, w_up, w_down, norm_final_g):
    split_idx = list(np.cumsum(IN_WIDTHS)[:-1])
    for _ in range(DEPTH):
        hn = rms_norm_2(x, norm_mix_g)
        z = hn @ w_in
        q_a, k_a, v_a, q_b, k_b, v_b, f_logit, g_a, g_b = jnp.split(z, split_idx, axis=-1)
        a = moba_attention(split_heads(q_a, N_HEADS_MOBA), split_heads(k_a, N_HEADS_MOBA),
                           split_heads(v_a, N_HEADS_MOBA))
        bfx = forgetting_attention(split_heads(q_b, N_HEADS_FOX), split_heads(k_b, N_HEADS_FOX),
                                   split_heads(v_b, N_HEADS_FOX), f_logit, b_forget)
        a = merge_heads_2(a) @ w_proj_a
        bfx = merge_heads_2(bfx) @ w_proj_b
        merged = jax.nn.sigmoid(g_a) * a + jax.nn.sigmoid(g_b) * bfx
        x = x + merged @ w_out
        hm = rms_norm_2(x, norm_mlp_g)
        x = x + jnp.square(jax.nn.relu(hm @ w_up)) @ w_down
    return rms_norm_2(x, norm_final_g)


def setup_inputs(seed=0):
    out = dict(first_inputs(seed))
    for name, value in second_inputs(seed + 1).items():
        if name != "x":
            out[name + "_2"] = value
    return out


def reference(
    x, c, ctx, c_ctx, w_ada, b_ada, g_mix_norm, w_in, g_q_a, w_q_b, g_kv_a, w_kv_b, conv_w,
    conv_b, g_mix_out, w_out, g_ffn_norm, w_up, ffn_conv_w, ffn_conv_b, w_down, g_final,
    norm_mix_g_2, w_in_2, b_forget_2, w_proj_a_2, w_proj_b_2, w_out_2, norm_mlp_g_2, w_up_2,
    w_down_2, norm_final_g_2,
):
    x = first_block(
        x, c, ctx, c_ctx, w_ada, b_ada, g_mix_norm, w_in, g_q_a, w_q_b, g_kv_a, w_kv_b, conv_w,
        conv_b, g_mix_out, w_out, g_ffn_norm, w_up, ffn_conv_w, ffn_conv_b, w_down, g_final,
    )
    return second_block(
        x, norm_mix_g_2, w_in_2, b_forget_2, w_proj_a_2, w_proj_b_2, w_out_2, norm_mlp_g_2,
        w_up_2, w_down_2, norm_final_g_2,
    )


_drawn_inputs = setup_inputs


def setup_inputs(seed=0):
    import zlib

    import numpy as np

    out = dict(_drawn_inputs(seed))
    spreads = {}
    factors = {'g_mix_norm': 3.826,
     'g_q_a': 8.0,
     'g_kv_a': 4.476,
     'conv_b': 8.0,
     'g_mix_out': 4.066,
     'g_ffn_norm': 3.989,
     'ffn_conv_b': 8.0,
     'norm_mix_g_2': 5.412,
     'norm_mlp_g_2': 3.272,
     'norm_final_g_2': 2.77}
    for name, (base, spread) in spreads.items():
        noise = np.random.default_rng([zlib.crc32(name.encode()), seed]).standard_normal(out[name].shape)
        drawn = base * np.exp(spread * noise) if base else spread * noise
        out[name] = __import__('jax').numpy.asarray(drawn.astype(out[name].dtype))
    for name, factor in factors.items():
        out[name] = (out[name] * factor).astype(out[name].dtype)
    return out
```

```python
from contextlib import ExitStack, contextmanager

import numpy as np

import concourse.bass as bass
from concourse import mybir

P = 128
D = 2048
T = 256
KT = D // P
TB = T // P
GW = 512
KC = 2
CW = KC * GW
GC = KT // KC
NRAW = 8
NSPLIT = 4
HEADS = 8
QR, KVR, ROPE = 512, 256, 64
FFN = 5504
FT = FFN // P
FF2 = 8192
HT = 16
EPS = 1e-6
MLA_SCALE = float((128 + 64) ** -0.5)
HEAD_SCALE = float(128 ** -0.5)
FAR = 1.0e30

F32 = mybir.dt.float32
F32R = mybir.dt.float32r
ACT = mybir.ActivationFunctionType
ALU = mybir.AluOpType
AX = mybir.AxisListType.X

VEC_GROUPS = [
    [("c", 16), ("c_ctx", 16), ("b_ada", 96)],
    [("g_mix_norm", 16), ("g_q_a", 4), ("g_kv_a", 2), ("conv_w", 24), ("conv_b", 8), ("g_mix_out", 16),
     ("g_ffn_norm", 16), ("g_final", 16), ("norm_mix_g_2", 16)],
    [("norm_mlp_g_2", 16), ("norm_final_g_2", 16), ("ffn_conv_b", 86)],
    [("ffn_conv_w0", 86)], [("ffn_conv_w1", 86)], [("ffn_conv_w2", 86)],
]
VEC_AT = {}
for _g, _names in enumerate(VEC_GROUPS):
    _r = 0
    for _name, _n in _names:
        VEC_AT[_name] = (_g, _r, _n)
        _r += _n
VEC_ROWS = [sum(n for _, n in names) for names in VEC_GROUPS]


def constants():
    c = {"ident": np.eye(P, dtype=np.float32)}
    sel = np.zeros((4, 2), np.float32)
    sel[[0, 2], 0] = 1
    sel[[1, 3], 1] = 1
    c["sel"] = sel
    t = np.arange(T)
    inv = (np.float32(10000.0) ** (-np.arange(0, 32, 2, dtype=np.float32) / np.float32(32))).astype(np.float32)
    row, col = (t // 64).astype(np.float32), (t % 64).astype(np.float32)
    ang = np.concatenate([row[:, None] * inv, col[:, None] * inv], axis=-1)
    cos, sin = np.cos(ang).astype(np.float32), np.sin(ang).astype(np.float32)
    d = np.arange(ROPE)
    sign = np.where(d % 2 == 0, -1.0, 1.0).astype(np.float32)
    c["rope"] = np.stack([cos[:, d // 2].T, sin[:, d // 2].T * sign[:, None]], 1).astype(np.float32).reshape(ROPE, 2 * T)
    swap = np.zeros((ROPE, ROPE), np.float32)
    swap[d, d ^ 1] = 1
    c["swap"] = swap
    q, k = np.arange(T)[:, None], np.arange(T)[None, :]
    blocks = lambda a: a.reshape(TB, P, T).transpose(1, 0, 2).reshape(P, TB * T).astype(np.float32)
    c["dist"] = blocks(np.where(q >= k, q - k, FAR))
    c["causal"] = blocks(np.where(q >= k, 0.0, -FAR))
    c["upto"] = blocks(q <= k)
    c["after"] = blocks(q > k)
    return {n: np.ascontiguousarray(a, np.float32) for n, a in c.items()}


class Ledger:

    def __init__(self, eng, name, known, traced):
        self.eng, self.name, self.known, self.traced = eng, name, known, traced
        self.n, self.loops, self.reg, self.per, self.trips = {}, 0, None, {}, 1

    def at(self, what, extra=0):
        base = self.n.get(what, 0) + extra
        return base + self.reg * self.per[what] if self.reg is not None and self.per.get(what) else base

    def add(self, what, k=1):
        self.n[what] = self.n.get(what, 0) + k

    def mark(self, sem, key=None):
        self.add(sem)
        if key is not None:
            assert (sem, key) not in self.traced, (sem, key)
            self.traced[sem, key] = (self.n[sem], self.per.get(sem, 0), self.trips if self.reg is not None else 1)

    def of(self, sem, key):
        value, per, trips = self.known.get((sem, key), (1, 0, 1))
        if self.reg is not None and self.trips == trips and per:
            return self.reg * per + value
        return value + per * (trips - 1)

    @contextmanager
    def loop(self, trips):
        start, me = dict(self.n), (self.name, self.loops)
        self.loops += 1
        self.per, self.trips = self.known.get(me, {}), trips
        with self.eng.Fori(0, trips) as i:
            self.reg = i
            yield i
        ring, slots = ("hi_ready", NSPLIT) if self.name == "pe" else ("drained", NRAW)
        assert (self.n.get("mod_summed", 0) - start.get("mod_summed", 0)) % 2 == 0
        assert (self.n.get(ring, 0) - start.get(ring, 0)) % slots == 0
        assert self.n.get("half_read", 0) % 2 == start.get("half_read", 0) % 2
        self.reg = None
        moved = {k: v - start.get(k, 0) for k, v in self.n.items() if v != start.get(k, 0)}
        self.traced[me] = moved
        for k, v in moved.items():
            self.n[k] = start.get(k, 0) + trips * v


class Stream(Ledger):

    end = 0

    def ended(self):
        per = self.per.get("hi_ready", 0) if self.reg is not None else 0
        return self.reg * per + self.end if per else self.end

    def raw_slot(self):
        return self.n.get("drained", 0) % NRAW

    def split_slot(self):
        return self.n.get("hi_ready", 0) % NSPLIT

    def loads(self):
        c = self.n.get("drained", 0)
        per = self.per.get("drained", 0) * 16 // NRAW if self.reg is not None else 0
        value = 16 * (c // NRAW + 1)
        return self.reg * per + value if per else value


STD = ("split", (CW,) * GC)
MOD = ("sum", (CW,) * GC)
KVG = ("split", (KC * (KVR + ROPE),) * GC)
QBG = ("split", (KC * 384,) * 2)
KVB = ("split", (CW,))
TAIL = ("split", (KC * 384,) * GC)
DN11 = ("split", (CW,) * 5 + (GW,))
FG = ("split", (KT * 8,))
PRJ = ("split", (CW,) * 4)
CONV_COLS = [at + GW * i for i in range(2) for at in (1856, 2880, 832)]
F_AT, GA_AT, GB_AT = 6144, 6152, 8200


def program(nc, ins, consts, out, known, traced):
    with ExitStack() as ctx:
        def sb(name, shape, dt=F32, scope=ctx):
            return scope.enter_context(nc.sbuf_tensor(name, shape, dt))

        raw_in = [ctx.enter_context(nc.semaphore(f"raw_in{i}")) for i in range(NRAW)]
        def sem(name):
            return ctx.enter_context(nc.semaphore(name))

        s_hi_ready = sem("hi_ready")
        s_drained = sem("drained")
        s_chunk_used = sem("chunk_used")
        s_half_read = sem("half_read")
        s_const_in = sem("const_in")
        s_vec_in = sem("vec_in")
        s_x_in = sem("x_in")
        s_rope_in = sem("rope_in")
        s_mask_in = sem("mask_in")
        s_bias_in = sem("bias_in")
        s_stored = sem("stored")
        s_filled = sem("filled")
        s_act_step = sem("act_step")
        s_dve_step = sem("dve_step")
        s_turned = sem("turned")
        s_summed = sem("summed")
        s_projected = sem("projected")
        s_silu = sem("silu")
        s_copied = sem("copied")
        s_squared = sem("squared")
        s_root = sem("root")
        s_rounded = sem("rounded")
        s_rounded_batch = sem("rounded_batch")
        s_tapped = sem("tapped")
        s_gated = sem("gated")
        s_columns = sem("columns")
        s_cst_ready = sem("cst_ready")
        s_row_ready = sem("row_ready")
        s_row_summed = sem("row_summed")
        s_mod_summed = sem("mod_summed")
        s_conved = sem("conved")
        s_batch = sem("batch")
        s_normed = sem("normed")
        s_act_lo = sem("act_lo")
        s_padded = sem("padded")
        s_stored_x = sem("stored_x")
        s_scores = sem("scores")
        s_maxed = sem("maxed")
        s_expd = sem("expd")
        s_probs = sem("probs")
        s_pt_turned = sem("pt_turned")
        s_pt_copied = sem("pt_copied")
        s_heads = sem("heads")
        s_heads_read = sem("heads_read")
        s_lf_ready = sem("lf_ready")
        s_lfw = sem("lfw")

        halves = [ctx.enter_context(nc.psum_tensor(f"half{i}", [P, 4, 512], F32)) for i in range(2)]

        def bank(i):
            return halves[i // 4][:, i % 4, :]

        xt = sb("xt", [P, KT, T])
        raw = sb("raw", [P, NRAW, CW])
        whi = sb("whi", [P, NSPLIT, CW], F32R)
        wlo = sb("wlo", [P, NSPLIT, CW], F32R)
        vec = sb("vec", [P, 6, P])
        ident = sb("ident_sb", [P, P])
        ones = sb("ones", [P, P])
        sel = sb("sel_sb", [4, 2])
        rstd = sb("rstd", [P, 2 * T])
        sq = sb("sq", [P, 2, 4 * T])
        tmp = sb("tmp", [P, 4, T])
        zpad = sb("zpad", [P, 4, T + 2])
        acc = sb("acc", [P, 2, GW])
        mod_a = sb("mod_a", [P, 32, 2])
        mod_f = sb("mod_f", [P, 64])
        gain = sb("gain", [P, KT, 3])
        silu = sb("silu_sb", [P, 32])
        stat = sb("stat", [P, 64])
        lf = sb("lf", [P, 6, TB, HEADS])
        bfb = sb("bfb", [P, HEADS])
        eps = sb("eps", [P, 1])

        first = ExitStack()
        t16 = sb("t16", [P, KT, T], scope=first)
        qraw = sb("qraw", [P, 4, T], scope=first)
        kvraw = sb("kvraw", [P, 2, 2 * T], scope=first)
        krope = sb("krope", [P, 2 * T], scope=first)
        sc = ExitStack()
        stage = sb("stage", [P, 4, D], scope=sc)
        cst = sb("cst", [P, KT, P], F32R, scope=sc)
        vrows = sb("vrows", [P, 6, P], scope=sc)
        row4 = sb("row4", [4, 2, GW], scope=sc)
        sc.close()
        sc = ExitStack()
        h1 = sb("h1", [P, KT, 2 * T], F32R, scope=sc)
        hctx = sb("hctx", [P, KT, 2 * T], F32R, scope=sc)
        sc.close()
        sc = ExitStack()
        rope = sb("rope_sb", [P, 2, T], scope=sc)
        swap = sb("swap_sb", [P, ROPE], scope=sc)
        qt = sb("qt", [P, HEADS, T], scope=sc)
        qrt = sb("qrt", [P, HEADS, T], scope=sc)
        ktt = sb("ktt", [P, HEADS, 2 * T], scope=sc)
        vt = sb("vt", [P, 4, HEADS * P], scope=sc)
        sc2 = ExitStack()
        qn = sb("qn", [P, 4, 2 * T], F32R, scope=sc2)
        kvn = sb("kvn", [P, 2, 4 * T], F32R, scope=sc2)
        sc2.close()
        sc2 = ExitStack()
        pr1 = sb("pr1", [P, 2, 2, 2 * T], scope=sc2)
        pt1 = sb("pt1", [P, 2, 4, T], scope=sc2)
        sc2.close()
        sc.close()
        sc = ExitStack()
        mix = sb("mix", [P, KT, 2 * T], F32R, scope=sc)
        sc.close()
        first.close()

        sc = ExitStack()
        hf = sb("hf", [P, KT, 2 * T], F32R, scope=sc)
        hid = [sb(f"hid{i}", [P, HT, 2 * T], F32R, scope=sc) for i in range(2)]
        sc.close()

        sc = ExitStack()
        heads2 = [sb(f"heads2_{i}", [P, HEADS, 2 * T], F32R, scope=sc) for i in range(2)]
        h2 = sb("h2", [P, KT, 2 * T], F32R, scope=sc)
        sc2 = ExitStack()
        q2 = sb("q2", [P, HEADS, T], scope=sc2)
        k2 = sb("k2", [P, HEADS, T], scope=sc2)
        v2 = sb("v2", [P, TB, HEADS * P], scope=sc2)
        dist = sb("dist_sb", [P, TB, T], scope=sc2)
        causal = sb("causal_sb", [P, TB, T], scope=sc2)
        upto = sb("upto_sb", [P, TB, T], scope=sc2)
        after = sb("after_sb", [P, TB, T], scope=sc2)
        sc2.close()
        sc2 = ExitStack()
        sigs = [sb(f"sig{i}", [P, KT, T], scope=sc2) for i in range(2)]
        sc2.close()
        sc.close()
        sc = ExitStack()
        outrow = sb("outrow", [P, TB, D], scope=sc)
        sc.close()

        p2 = sq[:, 0, :].rearrange("p (a b t) -> p a b t", a=2, b=2)
        pt2 = sq[:, 1, :].rearrange("p (a b t) -> p a b t", a=2, b=2)
        lfw = tmp[:, :, :].rearrange("p (a b) t -> p a b t", a=2)
        conv_y = [sq[:, i, :].rearrange("p (b t) -> p b t", b=4) for i in range(2)]

        def col(name, i=0):
            g, r, _ = VEC_AT[name]
            return vec[:, g, bass.ds(i + r, 1)]

        def cols(name, i, n):
            g, r, _ = VEC_AT[name]
            return vec[:, g, bass.ds(i + r, n)]

        W = {n: ins[n][0].rearrange("(k p) n -> p k n", p=P)
             for n in ("w_ada", "w_in", "w_q_b", "w_kv_b", "w_out", "w_up", "w_down")}
        W.update({n: ins[n].rearrange("(k p) n -> p k n", p=P)
                  for n in ("w_in_2", "w_proj_a_2", "w_proj_b_2", "w_out_2", "w_up_2", "w_down_2")})
        flat = lambda t: t[:].rearrange("p k t -> p (k t)")
        block = ctx.enter_context(nc.Block())

        @block.sync
        def _(sp):
            L = Stream(sp, "sp", known, traced)

            def load(w, k0, nk, c0, width):
                if L.n.get("drained", 0) >= NRAW:
                    sp.wait_ge(s_drained, L.at("drained", 1 - NRAW))
                dst = raw[:, L.raw_slot(), 0:nk * width].rearrange("p (k n) -> p k n", k=nk)
                sp.dma_start(dst, w[:, k0:k0 + nk, bass.ds(c0, width)]).then_inc(raw_in[L.raw_slot()], 16)
                L.add("drained")

            def group(name, c0, width=GW, k0=0, nk=KT):
                for k in range(k0, k0 + nk, KC):
                    load(W[name], k, min(KC, k0 + nk - k), c0, width)

            def groups(name, n, base=0, k0=0, nk=KT):
                with L.loop(n // 2) as i:
                    for g in range(2):
                        group(name, i * (2 * GW) + (base + g * GW), GW, k0, nk)

            sp.dma_start(ident[:], consts["ident"]).then_inc(s_const_in, 16)
            sp.dma_start(sel[:], consts["sel"]).then_inc(s_const_in, 16)
            for tb in range(TB):
                sp.dma_start(stage[:, tb, :], ins["x"][0, tb * P:(tb + 1) * P, :]).then_inc(s_x_in, 16)
            group("w_ada", 0)
            group("w_ada", GW)
            groups("w_ada", 6, 2 * GW)
            mod = 8 * GW
            group("w_in", QR, KVR + ROPE)
            group("w_in", 0)
            group("w_ada", mod)
            for n, at in enumerate(CONV_COLS):
                group("w_in", at)
                group("w_ada", mod + (n + 1) * GW)
            for g in range(4):
                group("w_q_b", g * 384, 384, 0, 4)
            group("w_ada", mod + 7 * GW)
            for g in range(4):
                group("w_kv_b", g * GW, GW, 0, KC)
            sp.wait_ge(s_act_lo, L.of("act_lo", ("kvn", 1)))
            sp.dma_start(rope[ROPE:P, :, :], consts["rope"].rearrange("p (a t) -> p a t", a=2)).then_inc(s_rope_in, 16)
            sp.dma_start(swap[ROPE:P, :], consts["swap"]).then_inc(s_rope_in, 16)
            with L.loop(2) as i:
                for g in range(2):
                    group("w_out", i * (2 * GW) + g * GW)
                    group("w_ada", i * (2 * GW) + (mod + 8 * GW + g * GW))
            with L.loop(2) as i:
                for g in range(2):
                    group("w_up", i * (2 * GW) + g * GW)
                    group("w_up", i * (2 * GW) + (g * GW + FFN))
                for g in range(2):
                    group("w_ada", i * (2 * GW) + (mod + 12 * GW + g * GW))

            def pairs(tile, n):
                with L.loop(n) as i:
                    group("w_up", i * GW + tile * P)
                    group("w_up", i * GW + (FFN + tile * P))

            pairs(HT, 4)
            groups("w_down", 4)
            pairs(2 * HT, 2)
            group("w_up", 40 * P, 3 * P)
            group("w_up", FFN + 40 * P, 3 * P)
            groups("w_down", 4, 0, HT)
            for g in range(4):
                group("w_down", g * GW, GW, 2 * HT, FT - 2 * HT)
            groups("w_in_2", 6)
            sp.wait_ge(s_act_lo, L.of("act_lo", ("h2", KT - 1)))
            for t, n in ((dist, "dist"), (causal, "causal"), (upto, "upto"), (after, "after")):
                sp.dma_start(t[:], consts[n].rearrange("p (a t) -> p a t", a=TB)).then_inc(s_mask_in, 16)
            groups("w_in_2", 6, 3072)
            load(W["w_in_2"], 0, KT, F_AT, 8)
            with L.loop(4) as i:
                group("w_in_2", i * GW + GA_AT)
                group("w_in_2", i * GW + GB_AT)
            with L.loop(4) as i:
                group("w_proj_a_2", i * GW, GW, 0, 8)
                group("w_proj_b_2", i * GW, GW, 0, 8)
            groups("w_out_2", 4)
            for f in range(5):
                if f < 4:
                    groups("w_up_2", 4, f * D)
                if f > 0:
                    groups("w_down_2", 4, 0, (f - 1) * HT)
            for tb in range(TB):
                sp.wait_ge(s_half_read, L.of("half_read", ("row", tb)))
                sp.dma_start(out[0, tb * P:(tb + 1) * P, :], outrow[:, tb, :]).then_inc(s_stored, 16)
            sp.wait_ge(s_stored, 16 * TB)

        @block.gpsimd
        def _(pool):
            L = Stream(pool, "pool", known, traced)
            nc.gpsimd.memset(eps[:], EPS).then_inc(s_filled, 1)
            L.mark("filled", "eps")
            nc.gpsimd.memset(ones[:], 1.0).then_inc(s_filled, 1)
            L.mark("filled", "ones")
            nc.gpsimd.memset(cst[:].bitcast(F32), 0.0).then_inc(s_filled, 1)
            L.mark("filled", "cst")
            nc.gpsimd.memset(zpad[:], 0.0).then_inc(s_filled, 1)
            L.mark("filled", "zpad")
            pool.wait_ge(s_lf_ready, L.of("lf_ready", "lf"))
            pool.wait_ge(s_mask_in, 64)
            for h in range(HEADS):
                if h >= 2:
                    pool.wait_ge(s_scores, L.of("scores", ("fox", h - 2, 1)))
                for s in range(TB):
                    nc.gpsimd.tensor_scalar(lfw[:, h % 2, s, :], upto[:, s, :], lf[:, 5, s, h:h + 1], None, ALU.mult)\
                        .then_inc(s_lfw, 1)
                    L.mark("lfw", (h, s))

        @block.scalar
        def _(act):
            L = Stream(act, "act", known, traced)
            A = nc.scalar.activation

            def split(elems):
                act.wait_ge(raw_in[L.raw_slot()], L.loads())
                if L.n.get("hi_ready", 0) >= NSPLIT:
                    act.wait_ge(s_chunk_used, L.at("hi_ready", 1 - NSPLIT))
                s, c = L.split_slot(), L.raw_slot()
                A(whi[:, s, 0:elems], raw[:, c, 0:elems], ACT.Copy).then_inc(s_hi_ready, 1)
                L.mark("hi_ready")
                L.add("drained")

            def ahead(group, between=None, later=None):
                L.end = L.n.get("hi_ready", 0)
                kind, chunks = group
                for n, elems in enumerate(chunks):
                    if n == 4 and between:
                        between()
                    if n == 6 and later:
                        later()
                    split(elems) if kind == "split" else L.add("drained")
                if len(chunks) <= 4 and between:
                    between()
                if len(chunks) <= 6 and later:
                    later()

            def done():
                act.wait_ge(s_chunk_used, L.ended())

            def second(nb=4, scale=1.0):
                act.wait_ge(s_half_read, L.at("half_read"))
                A(tmp[:, 0:nb, :], half()[:, 0:nb, T:2 * T], ACT.Copy, scale=scale).then_inc(s_copied, 1)
                L.mark("copied")

            def half():
                return halves[L.n.get("half_read", 0) % 2]

            def turn(k=1):
                L.add("half_read", k)

            def plain(scale=1.0):
                done()
                second(4, scale)
                turn()

            def squares(src, width=4 * T):
                act.wait_ge(s_half_read, L.at("half_read"))
                for j in range(src.shape[1] // width):
                    n = L.n.get("squared", 0)
                    if n >= 2:
                        act.wait_ge(s_summed, L.of("summed", ("sq", n - 2)))
                    A(sq[:, n % 2, 0:width], src[:, j * width:(j + 1) * width], ACT.Square).then_inc(s_squared, 1)
                    L.mark("squared", n)

            def root(n, dst, d):
                act.wait_ge(s_summed, L.of("summed", ("sq", L.n["squared"] - 1)))
                A(dst, half()[:, 0, 0:n], ACT.Sqrt, scale=1.0 / d, bias=eps[:]).then_inc(s_root, 1)
                L.mark("root", L.n["squared"])
                turn()

            def round_tiles(name, n, dst, shift=None):
                for k in range(n):
                    act.wait_ge(s_normed, L.of("normed", (name, k)))
                    t = tmp[:, k % 4, :]
                    ins_ = A(dst(k), t, ACT.Copy) if shift is None else A(dst(k), t, ACT.Identity, bias=shift(k))
                    ins_.then_inc(s_rounded, 1)
                    L.mark("rounded", (name, k))
                act.wait_ge(s_act_lo, L.of("act_lo", (name, n - 1)))

            def norm(name, src, dst, shift=None):
                squares(flat(src))
                root(T, rstd[:, 0:T], D)
                round_tiles(name, KT, lambda k: dst[:, k, 0:T], shift)

            row_src = {"c": ins["c"][0], "c_ctx": ins["c_ctx"]}
            for name in ("norm_mix_g_2", "norm_mlp_g_2", "norm_final_g_2", "g_final"):
                row_src[name] = ins[name]
            for name in ("b_ada", "g_mix_norm", "g_q_a", "g_kv_a", "g_mix_out", "conv_b", "g_ffn_norm", "ffn_conv_b"):
                row_src[name] = ins[name][0]
            for j in range(3):
                row_src[f"ffn_conv_w{j}"] = ins["ffn_conv_w"][0, j]
            row_src["conv_w"] = ins["conv_w"][0].rearrange("j n -> (j n)")
            for name, (g, r, n) in VEC_AT.items():
                act.dma_start(vrows[r:r + n, g, :], row_src[name].rearrange("(k p) -> k p", p=P)).then_inc(s_vec_in, 16)
            for tb in range(TB):
                act.dma_start(stage[:, 2 + tb, :], ins["ctx"][0, tb * P:(tb + 1) * P, :]).then_inc(s_x_in, 16)
            act.dma_start(bfb[:], ins["b_forget_2"].rearrange("(a n) -> a n", a=1).to_broadcast([P, HEADS]))\
                .then_inc(s_bias_in, 16)
            act.wait_ge(s_columns, L.of("columns", "vec"))
            turn()
            A(silu[:], vec[:, 0, 0:32], ACT.Silu).then_inc(s_silu, 1)
            L.mark("silu", "f32")
            act.wait_ge(s_silu, L.at("silu"))
            act.wait_ge(s_filled, L.of("filled", "cst"))
            A(cst[:, :, 0:2].rearrange("p k a -> p a k"), silu[:].rearrange("p (a k) -> p a k", a=2), ACT.Copy)\
                .then_inc(s_silu, 1)
            L.mark("silu", "hi")
            ahead(STD)
            turn(4)
            with L.loop(3):
                ahead(STD, turn)
                ahead(STD, turn)
            ahead(STD, turn)

            def norm_both():
                turn()
                act.wait_ge(s_columns, L.of("columns", "gain"))
                norm("h1", xt, h1, lambda k: mod_a[:, k, 0:1])
                norm("hctx", t16, hctx, lambda k: mod_a[:, k, 1:2])

            ahead(KVG, norm_both)

            def kv():
                done()
                for _ in range(2):
                    second(3)
                    turn()

            ahead(STD, kv)
            ahead(MOD, plain)
            for n in range(6):
                ahead(STD, turn)

                def conv(n=n):
                    plain()
                    if n % 3 == 1:
                        L.add("padded")
                        act.wait_ge(s_padded, L.at("padded"))
                        for b in range(4):
                            i = 4 * (n // 3) + b
                            A(conv_y[1][:, b, :], zpad[:, b, 1:T + 1], ACT.Identity,
                              scale=col("conv_w", 8 + i), bias=col("conv_b", i)).then_inc(s_tapped, 1)
                            L.mark("tapped", ("c", n, b))

                ahead(MOD, conv)

            def low_rank():
                turn()
                squares(flat(qraw))
                root(T, rstd[:, 0:T], QR)
                round_tiles("qn", 4, lambda k: qn[:, k, 0:T])
                squares(flat(kvraw))
                root(2 * T, rstd[:], KVR)
                for k in range(2):
                    act.wait_ge(s_normed, L.of("normed", ("kvn", k)))
                    A(kvn[:, k, :].rearrange("p (s a t) -> p s a t", s=2, a=2)[:, :, 0, :],
                      tmp[:, 2 * k:2 * k + 2, :], ACT.Copy).then_inc(s_rounded, 1)
                    L.mark("rounded", ("kvn", k))
                act.wait_ge(s_act_lo, L.of("act_lo", ("kvn", 1)))

            ahead(QBG, low_rank)
            for g in range(4):
                ahead(QBG if g < 3 else MOD, lambda: plain(MLA_SCALE))
            ahead(KVB, turn)
            def softmax(tag, h, qb, nk, src, dst, last=False):
                act.wait_ge(s_maxed, L.of("maxed", (tag, h, qb)))
                i = 2 * (h % 2) + qb
                A(dst, src, ACT.Exp, bias=stat[:, i:i + 1], accum_out=stat[:, 8 + i:9 + i]).then_inc(s_expd, 1)
                L.mark("expd", (tag, h, qb))

            def first_attention():
                turn(2)
                for h in range(HEADS + 1):
                    if h < HEADS:
                        for qb in range(TB):
                            softmax("mla", h, qb, 2 * T, bank(2 * (h % 2) + qb), pr1[:, h % 2, qb, :])
                    if h > 0:
                        g = h - 1
                        act.wait_ge(s_pt_turned, L.of("pt_turned", ("mla", g)))
                        A(pt1[:, g % 2, :, :], halves[1][:, 0:2, :].rearrange("p b (s t) -> p (b s) t", s=2),
                          ACT.Copy).then_inc(s_pt_copied, 1)
                        L.mark("pt_copied", ("mla", g))
                turn(2)
                act.wait_ge(s_half_read, L.at("half_read"))
                for j in range(4):
                    squares(flat(t16)[:, j * 4 * T:(j + 1) * 4 * T])
                for j in range(4):
                    act.wait_ge(s_summed, L.of("summed", ("sq", L.n["squared"] - 4 + j)))
                    src_ = halves[(L.n["half_read"] + j // 2) % 2][:, 2 * (j % 2):2 * (j % 2) + 2, :]
                    A(flat(tmp), src_.rearrange("p b n -> p (b n)"), ACT.Sqrt, scale=1.0 / P, bias=eps[:])\
                        .then_inc(s_root, 1)
                    L.mark("root", ("mix", j))
                    act.wait_ge(s_normed, L.of("normed", ("mix", j)))
                    for k in range(4 * j, 4 * j + 4):
                        A(mix[:, k, 0:T], t16[:, k, :], ACT.Copy, scale=col("g_mix_out", k)).then_inc(s_rounded, 1)
                        L.mark("rounded", ("mix", k))
                turn(2)


            for g in range(4):
                def kvb():
                    plain()
                    turn()
                ahead(KVB, kvb) if g < 3 else ahead(STD, lambda: (kvb(), first_attention()))

            def taps(name, i, b, out_, tag):
                A(out_, zpad[:, b, 1:T + 1], ACT.Identity, scale=col(name[0], i), bias=col(name[1], i))\
                    .then_inc(s_tapped, 1)
                L.mark("tapped")

            def up(side, tile, nb=4):
                done()
                second(nb)
                turn()
                act.wait_ge(s_half_read, L.at("half_read"))
                for b in range(nb):
                    taps(("ffn_conv_w1", "ffn_conv_b"), tile + (FT * side + b), b, conv_y[side][:, b, :], side)

            def gated(buf, tile, nb=4):
                L.add("conved", 2)
                act.wait_ge(s_conved, L.at("conved"))
                A(conv_y[1][:, 0:nb, :], conv_y[1][:, 0:nb, :], ACT.Silu).then_inc(s_gated, 1)
                L.mark("gated")
                round_batch(hid[buf], tile, nb)

            def round_batch(dst, tile, nb=4):
                L.add("batch")
                act.wait_ge(s_batch, L.at("batch"))
                A(dst[:, bass.ds(tile, nb), 0:T], conv_y[1][:, 0:nb, :], ACT.Copy).then_inc(s_rounded_batch, 1)
                L.mark("rounded_batch")

            for _ in range(3):
                ahead(MOD, turn)
                ahead(STD, turn)
            ahead(MOD, turn)
            ahead(STD, lambda: (turn(), norm("hf", xt, hf, lambda k: mod_f[:, 16 + k:17 + k])))
            with L.loop(2) as i:
                for g in range(2):
                    t = i * 8 + 4 * g
                    ahead(STD, lambda: up(0, t))
                    ahead(STD if g == 0 else MOD, lambda: up(1, t), lambda: gated(0, t))
                ahead(MOD, turn)
                ahead(STD, turn)
            with L.loop(4) as i:
                ahead(STD, lambda: up(0, i * 4 + HT))
                ahead(STD, lambda: up(1, i * 4 + HT), lambda: gated(1, i * 4))
            with L.loop(2):
                ahead(STD, turn)
                ahead(STD, turn)
            for j in range(3):
                nb = 4 if j < 2 else 3
                nxt = STD if j == 0 else TAIL
                ahead(TAIL if j == 2 else STD, lambda: up(0, 2 * HT + 4 * j, nb))
                ahead(STD if j != 1 else TAIL, lambda: up(1, 2 * HT + 4 * j, nb), lambda: gated(0, 4 * j, nb))
            for g in range(4):
                ahead(STD if g < 3 else DN11, turn)

            def two_norms():
                turn()
                squares(flat(xt))
                root(T, rstd[:, 0:T], D)
                act.wait_ge(s_stored_x, L.of("stored_x", "g_final"))
                norm("h2", xt, h2)

            for g in range(4):
                ahead(DN11 if g < 3 else STD, turn if g < 3 else two_norms)

            def second_attention(tag, dst):
                for h in range(HEADS + 2):
                    if h > 1:
                        g = h - 2
                        act.wait_ge(s_heads, L.of("heads", (tag, g)))
                        A(dst[:, g, 0:T], bank(6 + g % 2)[:, 0:T], ACT.Copy).then_inc(s_rounded, 1)
                        L.mark("rounded", (tag, g))
                    if h < HEADS:
                        for qb in range(TB):
                            p = p2[:, h % 2, qb, 0:(qb + 1) * P]
                            softmax(tag, h, qb, 0, p, p)
                    if 0 < h <= HEADS:
                        g = h - 1
                        act.wait_ge(s_pt_turned, L.of("pt_turned", (tag, g)))
                        A(pt2[:, g % 2, :, :].rearrange("p a t -> p (a t)")[:, 0:3 * P], bank(4)[:, 0:3 * P], ACT.Copy)\
                            .then_inc(s_pt_copied, 1)
                        L.mark("pt_copied", (tag, g))
                turn(2)

            def gates():
                act.wait_ge(s_half_read, L.at("half_read"))
                A(lf[:, 1], lf[:, 0], ACT.Abs).then_inc(s_act_step, 1)
                L.mark("act_step")
                act.wait_ge(s_act_step, L.at("act_step"))
                A(lf[:, 2], lf[:, 1], ACT.Exp, scale=-1.0).then_inc(s_act_step, 1)
                L.mark("act_step")
                act.wait_ge(s_act_step, L.at("act_step"))
                A(lf[:, 3], lf[:, 2], ACT.Ln, bias=1.0).then_inc(s_gated, 1)
                L.mark("gated", "lf")

            for branch in range(2):
                for g in range(4):
                    ahead(STD, lambda: plain(HEAD_SCALE if g < 2 else 1.0))
                ahead(STD, turn)
                if branch == 0:
                    ahead(STD, lambda: (turn(), second_attention("alibi", heads2[0])))
                else:
                    ahead(FG, turn)
                    ahead(STD, lambda: (turn(), gates(), second_attention("fox", heads2[1])))

            def gate(side, i):
                plain()
                act.wait_ge(s_half_read, L.at("half_read"))
                t = sigs[side][:, bass.ds(i * 4, 4), :]
                A(t, t, ACT.Sigmoid).then_inc(s_gated, 1)
                L.mark("gated")

            with L.loop(3) as i:
                ahead(STD, lambda: gate(0, i))
                ahead(STD, lambda: gate(1, i))
            ahead(STD, lambda: gate(0, 3))
            ahead(PRJ, lambda: gate(1, 3))
            with L.loop(3) as i:
                ahead(PRJ, plain)
                ahead(PRJ, lambda: (plain(), round_batch(h2, i * 4)))
            ahead(PRJ, plain)
            ahead(STD, lambda: (plain(), round_batch(h2, 12)))
            for g in range(4):
                ahead(STD, turn if g < 3 else (lambda: (turn(), norm("hm", xt, hf))))
            for f in range(5):
                if f < 4:
                    with L.loop(2) as i:
                        for g in range(2):
                            ahead(STD, lambda: (plain(), round_batch(hid[f % 2], i * 8 + 4 * g)))
                if 0 < f < 4:
                    with L.loop(2):
                        ahead(STD, turn)
                        ahead(STD, turn)
            for g in range(3):
                ahead(STD, turn)
            turn()
            squares(flat(xt))
            root(T, rstd[:, 0:T], D)

        @block.vector
        def _(dve):
            L = Stream(dve, "dve", known, traced)
            V = nc.vector

            def split(elems):
                s, c = L.split_slot(), L.raw_slot()
                L.add("hi_ready")
                dve.wait_ge(s_hi_ready, L.at("hi_ready"))
                V.tensor_tensor(wlo[:, s, 0:elems], raw[:, c, 0:elems], whi[:, s, 0:elems].bitcast(F32),
                                ALU.subtract).then_inc(s_drained, 1)
                L.mark("drained")

            def sum_chunk(j):
                dve.wait_ge(raw_in[L.raw_slot()], L.loads())
                a = acc[:, L.n.get("acc_ready", 0) % 2, :]
                if j == 0 and L.n.get("acc_ready", 0) >= 2:
                    dve.wait_ge(s_mod_summed, L.at("acc_ready", -1))
                for k in range(KC):
                    w, s = raw[:, L.raw_slot(), k * GW:(k + 1) * GW], silu[:, KC * j + k:KC * j + k + 1]
                    ins_ = V.tensor_scalar(a, w, s, None, ALU.mult) if j + k == 0 else \
                        V.scalar_tensor_tensor(a, w, s, a, ALU.mult, ALU.add)
                    if k < KC - 1:
                        ins_.then_inc(s_dve_step, 1)
                        L.mark("dve_step")
                        dve.wait_ge(s_dve_step, L.at("dve_step"))
                    else:
                        ins_.then_inc(s_drained, 1)
                        L.mark("drained")
                        dve.wait_ge(s_drained, L.at("drained"))
                if j == GC - 1:
                    L.add("acc_ready")

            def ahead(group, between=None, later=None):
                L.end = L.n.get("hi_ready", 0)
                kind, chunks = group
                for n, elems in enumerate(chunks):
                    if n == 4 and between:
                        between()
                    if n == 6 and later:
                        later()
                    split(elems) if kind == "split" else sum_chunk(n)
                if len(chunks) <= 4 and between:
                    between()
                if len(chunks) <= 6 and later:
                    later()

            def half():
                return halves[L.n.get("half_read", 0) % 2]

            def tt(o, a, b, op=ALU.add):
                return V.tensor_tensor(o, a, b, op)

            def copied():
                L.add("copied")
                dve.wait_ge(s_copied, L.at("copied"))

            def halves_sum(dst, nb=4, scale=1.0):
                copied()
                first = half()[:, 0:nb, 0:T]
                if scale == 1.0:
                    tt(dst, first, tmp[:, 0:nb, :]).then_inc(s_half_read, 1)
                    L.mark("half_read")
                else:
                    V.scalar_tensor_tensor(dst, first, scale, tmp[:, 0:nb, :], ALU.mult, ALU.add).then_inc(s_half_read, 1)
                    L.mark("half_read")

            def inverse(n):
                L.add("norm")
                dve.wait_ge(s_root, L.of("root", L.n["squared"]))
                V.reciprocal(rstd[:, 0:n], rstd[:, 0:n]).then_inc(s_half_read, 1)
                L.mark("half_read")
                dve.wait_ge(s_half_read, L.at("half_read"))

            def norm(name, n, src, gain_of, dst, shift=None):
                def lo(k):
                    dve.wait_ge(s_rounded, L.of("rounded", (name, k)))
                    t, hi = tmp[:, k % 4, :], dst[:, k, 0:T].bitcast(F32)
                    ins_ = tt(dst[:, k, T:2 * T], t, hi, ALU.subtract) if shift is None else \
                        V.scalar_tensor_tensor(dst[:, k, T:2 * T], t, shift(k), hi, ALU.add, ALU.subtract)
                    ins_.then_inc(s_act_lo, 1)
                    L.mark("act_lo", (name, k))

                for k in range(n + 2):
                    if k < n:
                        if k >= 4:
                            dve.wait_ge(s_act_lo, L.at("act_lo", -1))
                        V.scalar_tensor_tensor(tmp[:, k % 4, :], src[:, k, :], gain_of(k), rstd[:, 0:T],
                                               ALU.mult, ALU.mult).then_inc(s_normed, 1)
                        L.mark("normed", (name, k))
                    if k >= 2:
                        lo(k - 2)

            def square_count(k):
                L.add("squared", k)

            dve.wait_ge(s_turned, L.of("turned", "vec"))
            V.tensor_copy(vec[:, 0, :], half()[:, 0, 0:P]).then_inc(s_columns, 1)
            L.mark("columns", "vec")
            n1, n3 = VEC_ROWS[1], VEC_ROWS[3]
            hv = half()[:, 0:2, :].rearrange("p b (g n) -> p b g n", n=P)
            V.tensor_copy(vec[:, 1:3, 0:n1], hv[:, 0, 1:3, 0:n1]).then_inc(s_columns, 1)
            L.mark("columns")
            V.tensor_copy(vec[:, 3:6, 0:n3], hv[:, 1, 0:3, 0:n3]).then_inc(s_half_read, 1)
            L.mark("half_read")
            dve.wait_ge(s_silu, L.of("silu", "hi"))
            tt(cst[:, :, 2:4].rearrange("p k a -> p a k"), silu[:].rearrange("p (a k) -> p a k", a=2),
               cst[:, :, 0:2].bitcast(F32).rearrange("p k a -> p a k"), ALU.subtract).then_inc(s_cst_ready, 1)
            L.mark("cst_ready", "lo")
            for tb in range(4):
                dve.wait_ge(s_turned, L.of("turned", tb))
                dst = (xt if tb < 2 else t16)[:, :, (tb % 2) * P:(tb % 2 + 1) * P]
                V.tensor_copy(dst, half()[:].rearrange("p b (k t) -> p (b k) t", t=P)).then_inc(s_half_read, 1)
                L.mark("half_read")
            ahead(STD)

            def mod_rows(j):
                dve.wait_ge(s_chunk_used, L.ended())
                s = L.n.get("row_ready", 0) % 2
                V.tensor_copy(row4[:, s, :], half()[0:4, 0, :]).then_inc(s_row_ready, 1)
                L.mark("row_ready")
                L.add("row_summed")
                dve.wait_ge(s_row_summed, L.at("row_summed"))
                b = cols("b_ada", j, 4).rearrange("p (a n) -> p n a", a=1).to_broadcast([P, 4, 2])
                tt(mod_a[:, bass.ds(j, 4), :], half()[:, 1, 0:8].rearrange("p (n a) -> p n a", a=2), b)\
                    .then_inc(s_half_read, 1)
                L.mark("half_read")

            with L.loop(3) as i:
                ahead(STD, lambda: mod_rows(i * 8))
                ahead(STD, lambda: mod_rows(i * 8 + 4))
            ahead(STD, lambda: mod_rows(24))

            def norm_both():
                mod_rows(28)
                dve.wait_ge(s_half_read, L.at("half_read"))
                for n in range(2):
                    V.scalar_tensor_tensor(gain[:, :, n], mod_a[:, 16:32, n], 1.0, cols("g_mix_norm", 0, 16),
                                           ALU.add, ALU.mult).then_inc(s_columns, 1)
                    L.mark("columns", "gain" if n else None)
                dve.wait_ge(s_columns, L.at("columns"))
                square_count(4)
                inverse(T)
                norm("h1", KT, xt, lambda k: gain[:, k, 0:1], h1, lambda k: mod_a[:, k, 0:1])
                square_count(4)
                inverse(T)
                norm("hctx", KT, t16, lambda k: gain[:, k, 1:2], hctx, lambda k: mod_a[:, k, 1:2])

            ahead(KVG, norm_both)

            def kv():
                for s in range(2):
                    copied()
                    at = slice(s * T, (s + 1) * T)
                    tt(kvraw[:, :, at], half()[:, 0:2, 0:T], tmp[:, 0:2, :]).then_inc(s_dve_step, 1)
                    L.mark("dve_step")
                    tt(krope[ROPE:P, at], half()[ROPE:P, 2, 0:T], tmp[ROPE:P, 2, :]).then_inc(s_half_read, 1)
                    L.mark("half_read")

            ahead(STD, kv)
            ahead(MOD, lambda: halves_sum(qraw[:]))

            def mod(j):
                L.add("mod_summed")
                dve.wait_ge(s_mod_summed, L.at("mod_summed"))
                tt(mod_f[:, bass.ds(j, 4)], half()[:, 0, 0:4], cols("b_ada", j + 32, 4)).then_inc(s_half_read, 1)
                L.mark("half_read")

            def outer_taps(names, i, y, nb=4):
                for b in range(nb):
                    L.add("tapped")
                    dve.wait_ge(s_tapped, L.at("tapped"))
                    V.scalar_tensor_tensor(y[:, b, :], zpad[:, b, 0:T], col(names[0], i + b), y[:, b, :],
                                           ALU.mult, ALU.add).then_inc(s_dve_step, 1)
                    L.mark("dve_step")
                dve.wait_ge(s_dve_step, L.at("dve_step"))
                for b in range(nb):
                    ins_ = V.scalar_tensor_tensor(y[:, b, :], zpad[:, b, 2:T + 2], col(names[1], i + b), y[:, b, :],
                                                  ALU.mult, ALU.add)
                ins_.then_inc(s_conved, 1)
                L.mark("conved")

            dve.wait_ge(s_filled, L.of("filled", "zpad"))
            for n in range(6):
                ahead(STD, lambda: mod(4 * n))

                def conv():
                    if n % 3 == 0:
                        halves_sum(conv_y[0])
                    elif n % 3 == 1:
                        halves_sum(zpad[:, :, 1:T + 1])
                        dve.wait_ge(s_half_read, L.at("half_read"))
                        tt(zpad[:, :, 1:T + 1], zpad[:, :, 1:T + 1], conv_y[0], ALU.mult).then_inc(s_padded, 1)
                        L.mark("padded", (n, 3))
                        i = 4 * (n // 3)
                        dve.wait_ge(s_padded, L.at("padded"))
                        for b in range(4):
                            dve.wait_ge(s_tapped, L.of("tapped", ("c", n, b)))
                            L.add("tapped")
                            V.scalar_tensor_tensor(conv_y[1][:, b, :], zpad[:, b, 0:T], col("conv_w", i + b),
                                                   conv_y[1][:, b, :], ALU.mult, ALU.add).then_inc(s_dve_step, 1)
                            L.mark("dve_step")
                        dve.wait_ge(s_dve_step, L.at("dve_step"))
                        for b in range(4):
                            V.scalar_tensor_tensor(conv_y[1][:, b, :], zpad[:, b, 2:T + 2], col("conv_w", 16 + i + b),
                                                   conv_y[1][:, b, :], ALU.mult, ALU.add).then_inc(s_dve_step, 1)
                            L.mark("dve_step")
                    else:
                        dst = t16[:, 8 + 4 * (n // 3):12 + 4 * (n // 3), :]
                        halves_sum(dst)
                        dve.wait_ge(s_half_read, L.at("half_read"))
                        dve.wait_ge(s_dve_step, L.at("dve_step"))
                        tt(dst, dst, conv_y[1], ALU.mult).then_inc(s_stored_x, 1)
                        L.mark("stored_x", ("conv", n))

                ahead(MOD, conv)

            def low_rank():
                mod(24)
                square_count(1)
                inverse(T)
                norm("qn", 4, qraw, lambda k: col("g_q_a", k), qn)
                square_count(1)
                inverse(2 * T)
                for k in range(2):
                    V.scalar_tensor_tensor(tmp[:, 2 * k:2 * k + 2, :], kvraw[:, k, :].rearrange("p (s t) -> p s t", s=2),
                                           col("g_kv_a", k), rstd[:].rearrange("p (s t) -> p s t", s=2),
                                           ALU.mult, ALU.mult).then_inc(s_normed, 1)
                    L.mark("normed", ("kvn", k))
                for k in range(2):
                    dve.wait_ge(s_rounded, L.of("rounded", ("kvn", k)))
                    v = kvn[:, k, :].rearrange("p (s a t) -> p s a t", s=2, a=2)
                    tt(v[:, :, 1, :], tmp[:, 2 * k:2 * k + 2, :], v[:, :, 0, :].bitcast(F32), ALU.subtract)\
                        .then_inc(s_act_lo, 1)
                    L.mark("act_lo", ("kvn", k))

            ahead(QBG, low_rank)
            for g in range(4):
                def qb():
                    copied()
                    V.scalar_tensor_tensor(qt[:, 2 * g:2 * g + 2, :], half()[:, 0:4:2, 0:T], MLA_SCALE,
                                           tmp[:, 0:4:2, :], ALU.mult, ALU.add).then_inc(s_dve_step, 1)
                    L.mark("dve_step")
                    V.scalar_tensor_tensor(qrt[ROPE:P, 2 * g:2 * g + 2, :], half()[ROPE:P, 1:4:2, 0:T], MLA_SCALE,
                                           tmp[ROPE:P, 1:4:2, :], ALU.mult, ALU.add).then_inc(s_half_read, 1)
                    L.mark("half_read", ("q", g))
                ahead(QBG if g < 3 else MOD, qb)
            ahead(KVB, lambda: mod(28))

            def rotate():
                dve.wait_ge(s_rope_in, 32)
                dve.wait_ge(s_projected, L.of("projected", "q"))
                cosine = rope[ROPE:P, 0:1, :].to_broadcast([ROPE, HEADS, T])
                sine = rope[ROPE:P, 1:2, :].to_broadcast([ROPE, HEADS, T])
                s = sq[ROPE:P, :, :].rearrange("p a (h t) -> p (a h) t", t=T)
                tt(qrt[ROPE:P], qrt[ROPE:P], cosine, ALU.mult).then_inc(s_dve_step, 1)
                L.mark("dve_step")
                tt(s, half()[ROPE:P].rearrange("p b (h t) -> p (b h) t", t=T), sine, ALU.mult).then_inc(s_half_read, 1)
                L.mark("half_read")
                dve.wait_ge(s_half_read, L.at("half_read"))
                dve.wait_ge(s_dve_step, L.at("dve_step"))
                tt(qrt[ROPE:P], qrt[ROPE:P], s).then_inc(s_stored_x, 1)
                L.mark("stored_x", "qrt")
                dve.wait_ge(s_stored_x, L.at("stored_x"))
                dve.wait_ge(s_projected, L.of("projected", "k"))
                tt(krope[ROPE:P, 0:T], krope[ROPE:P, 0:T], rope[ROPE:P, 0, :], ALU.mult).then_inc(s_dve_step, 1)
                L.mark("dve_step")
                tt(s[:, 0, :], half()[ROPE:P, 0, 0:T], rope[ROPE:P, 1, :], ALU.mult).then_inc(s_half_read, 1)
                L.mark("half_read")
                dve.wait_ge(s_half_read, L.at("half_read"))
                dve.wait_ge(s_dve_step, L.at("dve_step"))
                tt(krope[ROPE:P, 0:T], krope[ROPE:P, 0:T], s[:, 0, :]).then_inc(s_stored_x, 1)
                L.mark("stored_x", "krope")

            def weigh(tag, g, probs):
                for qb in range(TB):
                    i = 2 * (g % 2) + qb
                    dve.wait_ge(s_expd, L.of("expd", (tag, g, qb)))
                    V.reciprocal(stat[:, 16 + i:17 + i], stat[:, 8 + i:9 + i]).then_inc(s_dve_step, 1)
                    L.mark("dve_step")
                    dve.wait_ge(s_dve_step, L.at("dve_step"))
                    p = probs(qb)
                    V.tensor_scalar(p, p, stat[:, 16 + i:17 + i], None, ALU.mult).then_inc(s_probs, 1)
                    L.mark("probs", (tag, g, qb))

            def first_attention():
                rotate()
                for h in range(HEADS + 2):
                    if h < HEADS:
                        for qb in range(TB):
                            dve.wait_ge(s_scores, L.of("scores", ("mla", h, qb)))
                            i = 2 * (h % 2) + qb
                            V.tensor_reduce(stat[:, i:i + 1], bank(i), AX, ALU.max, negate=True).then_inc(s_maxed, 1)
                            L.mark("maxed", ("mla", h, qb))
                    if 0 < h <= HEADS:
                        weigh("mla", h - 1, lambda qb: pr1[:, (h - 1) % 2, qb, :])
                    if h > 1:
                        g = h - 2
                        dve.wait_ge(s_heads, L.of("heads", ("mla", g)))
                        ins_ = V.tensor_copy(t16[:, g, :], bank(6 + g % 2)[:, 0:T])
                        ins_.then_inc(s_heads_read, 1)
                        L.mark("heads_read", ("mla", g))
                dve.wait_ge(s_heads_read, L.at("heads_read"))
                V.memset(stat[:, 32:33], 0.0).then_inc(s_half_read, 1)
                L.mark("half_read")
                V.memset(stat[:, 33:34], 0.0).then_inc(s_half_read, 1)
                L.mark("half_read", "mla done")
                square_count(4)
                for j in range(4):
                    dve.wait_ge(s_root, L.of("root", ("mix", j)))
                    ins_ = V.reciprocal(flat(tmp), flat(tmp))
                    if j % 2 == 0:
                        ins_.then_inc(s_dve_step, 1)
                        L.mark("dve_step")
                        dve.wait_ge(s_dve_step, L.at("dve_step"))
                    else:
                        ins_.then_inc(s_half_read, 1)
                        L.mark("half_read")
                        dve.wait_ge(s_half_read, L.at("half_read"))
                    ks = slice(4 * j, 4 * j + 4)
                    tt(t16[:, ks, :], t16[:, ks, :], tmp[:], ALU.mult).then_inc(s_normed, 1)
                    L.mark("normed", ("mix", j))
                    dve.wait_ge(s_normed, L.at("normed"))
                    for k in range(4 * j, 4 * j + 4):
                        dve.wait_ge(s_rounded, L.of("rounded", ("mix", k)))
                        V.scalar_tensor_tensor(mix[:, k, T:2 * T], t16[:, k, :], col("g_mix_out", k),
                                               mix[:, k, 0:T].bitcast(F32), ALU.mult, ALU.subtract).then_inc(s_act_lo, 1)
                        L.mark("act_lo", ("mix", k))

            for g in range(4):
                def kvb():
                    heads = ktt[:, 2 * g:2 * g + 2, :].rearrange("p h (s t) -> p (h s) t", s=2)
                    halves_sum(heads)
                    dve.wait_ge(s_chunk_used, L.ended())
                    V.tensor_copy(vt[:, :, g * 2 * P:(g + 1) * 2 * P],
                                  half()[:, 0:2, :].rearrange("p b (s n) -> p (b s) n", s=2)).then_inc(s_half_read, 1)
                    L.mark("half_read", ("kv", g))
                ahead(KVB, kvb) if g < 3 else ahead(STD, lambda: (kvb(), first_attention()))

            def onto_x(t, gate_of=None):
                dve.wait_ge(s_chunk_used, L.ended())
                for part in range(2):
                    src = half()[:, :, part * T:(part + 1) * T]
                    if gate_of is None:
                        x4 = xt[:, bass.ds(t, 4), :]
                        ins_ = [tt(x4, src, x4)]
                    else:
                        for b in range(4):
                            xb = xt[:, bass.ds(t + b, 1), :].rearrange("p a t -> p (a t)")
                            one = V.scalar_tensor_tensor(xb, src[:, b, :], gate_of(t + b), xb, ALU.mult, ALU.add)
                            if b < 3:
                                one.then_inc(s_dve_step, 1)
                                L.mark("dve_step")
                        ins_ = [one]
                    if part == 0:
                        ins_[0].then_inc(s_dve_step, 1)
                        L.mark("dve_step")
                        dve.wait_ge(s_dve_step, L.at("dve_step"))
                    else:
                        ins_[0].then_inc(s_half_read, 1)
                        L.mark("half_read")

            def mix_gate(t):
                return mod_f[:, bass.ds(t, 1)]

            def ffn_gate(t):
                return mod_f[:, bass.ds(t + 48, 1)]

            for g in range(3):
                ahead(MOD, lambda: onto_x(g * 4, mix_gate))
                ahead(STD, lambda: mod(g * 4 + 32))
            ahead(MOD, lambda: onto_x(12, mix_gate))

            def ffn_norm():
                mod(44)
                dve.wait_ge(s_half_read, L.at("half_read"))
                V.scalar_tensor_tensor(gain[:, :, 2], mod_f[:, 32:48], 1.0, cols("g_ffn_norm", 0, 16),
                                       ALU.add, ALU.mult).then_inc(s_columns, 1)
                L.mark("columns", "ffn gain")
                dve.wait_ge(s_columns, L.at("columns"))
                square_count(4)
                inverse(T)
                norm("hf", KT, xt, lambda k: gain[:, k, 2:3], hf, lambda k: mod_f[:, 16 + k:17 + k])

            ahead(STD, ffn_norm)

            def up(side, tile, nb=4):
                copied()
                tt(zpad[:, 0:nb, 1:T + 1], half()[:, 0:nb, 0:T], tmp[:, 0:nb, :]).then_inc(s_half_read, 1)
                L.mark("half_read")
                outer_taps(("ffn_conv_w0", "ffn_conv_w2"), tile + FT * side, conv_y[side], nb)

            def gated(buf, tile, nb=4, key=None):
                L.add("gated")
                dve.wait_ge(s_gated, L.at("gated"))
                dve.wait_ge(s_conved, L.at("conved"))
                y = conv_y[1][:, 0:nb, :]
                tt(y, y, conv_y[0][:, 0:nb, :], ALU.mult).then_inc(s_batch, 1)
                L.mark("batch")
                dve.wait_ge(s_batch, L.at("batch"))
                lo_batch(hid[buf], tile, nb, key)

            def lo_batch(dst, tile, nb=4, key=None):
                L.add("rounded_batch")
                dve.wait_ge(s_rounded_batch, L.at("rounded_batch"))
                tt(dst[:, bass.ds(tile, nb), T:2 * T], conv_y[1][:, 0:nb, :],
                   dst[:, bass.ds(tile, nb), 0:T].bitcast(F32), ALU.subtract).then_inc(s_act_lo, 1)
                L.mark("act_lo", key)

            with L.loop(2) as i:
                for g in range(2):
                    t = i * 8 + 4 * g
                    ahead(STD, lambda: up(0, t))
                    ahead(STD if g == 0 else MOD, lambda: up(1, t), lambda: gated(0, t, 4, ("hid", 0) if g else None))
                ahead(MOD, lambda: mod(i * 8 + 48))
                ahead(STD, lambda: mod(i * 8 + 52))
            with L.loop(4) as i:
                ahead(STD, lambda: up(0, i * 4 + HT))
                ahead(STD, lambda: up(1, i * 4 + HT), lambda: gated(1, i * 4, 4, ("hid", 1)))
            with L.loop(2) as i:
                for g in range(2):
                    ahead(STD, lambda: onto_x(i * 8 + 4 * g, ffn_gate))
            for j in range(3):
                nb = 4 if j < 2 else 3
                ahead(TAIL if j == 2 else STD, lambda: up(0, 2 * HT + 4 * j, nb))
                ahead(STD if j != 1 else TAIL, lambda: up(1, 2 * HT + 4 * j, nb),
                      lambda: gated(0, 4 * j, nb, ("hid", 2) if j == 2 else None))
            for g in range(4):
                ahead(STD if g < 3 else DN11, lambda: onto_x(4 * g, ffn_gate))

            def norm_onto_x(name):
                square_count(4)
                inverse(T)
                for k in range(KT):
                    V.scalar_tensor_tensor(xt[:, k, :], xt[:, k, :], col(name, k), rstd[:, 0:T], ALU.mult, ALU.mult)\
                        .then_inc(s_stored_x, 1)
                    L.mark("stored_x", name if k == KT - 1 else None)

            def norm_h2():
                norm_onto_x("g_final")
                square_count(4)
                dve.wait_ge(s_stored_x, L.at("stored_x"))
                inverse(T)
                norm("h2", KT, xt, lambda k: col("norm_mix_g_2", k), h2)

            for g in range(4):
                ahead(DN11 if g < 3 else STD,
                      lambda: (onto_x(4 * g, ffn_gate), norm_h2() if g == 3 else None))

            def second_attention(tag, dst):
                if tag == "alibi":
                    dve.wait_ge(s_mask_in, 64)
                for h in range(HEADS + 2):
                    if h > 1:
                        g = h - 2
                        dve.wait_ge(s_rounded, L.of("rounded", (tag, g)))
                        tt(dst[:, g, T:2 * T], bank(6 + g % 2)[:, 0:T], dst[:, g, 0:T].bitcast(F32), ALU.subtract)\
                            .then_inc(s_act_lo, 1)
                        L.mark("act_lo", (tag, g))
                    if h < HEADS:
                        for qb in range(TB):
                            dve.wait_ge(s_scores, L.of("scores", (tag, h, qb)))
                            i, nk = 2 * (h % 2) + qb, (qb + 1) * P
                            p = p2[:, h % 2, qb, 0:nk]
                            if tag == "alibi":
                                ins_ = V.scalar_tensor_tensor(p, dist[:, qb, 0:nk], -(2.0 ** -(h + 1)), bank(i)[:, 0:nk],
                                                              ALU.mult, ALU.add)
                            else:
                                ins_ = tt(p, causal[:, qb, 0:nk], bank(i)[:, 0:nk])
                            ins_.then_inc(s_dve_step, 1)
                            L.mark("dve_step")
                            dve.wait_ge(s_dve_step, L.at("dve_step"))
                            V.tensor_reduce(stat[:, i:i + 1], p, AX, ALU.max, negate=True).then_inc(s_maxed, 1)
                            L.mark("maxed", (tag, h, qb))
                    if 0 < h <= HEADS:
                        weigh(tag, h - 1, lambda qb: p2[:, (h - 1) % 2, qb, 0:(qb + 1) * P])
                dve.wait_ge(s_act_lo, L.at("act_lo"))
                V.memset(stat[:, 32:33], 0.0).then_inc(s_half_read, 1)
                L.mark("half_read")
                V.memset(stat[:, 33:34], 0.0).then_inc(s_half_read, 1)
                L.mark("half_read", (tag, "done"))

            def values(g):
                dve.wait_ge(s_chunk_used, L.ended())
                V.tensor_copy(v2[:, :, g * GW:(g + 1) * GW], half()[:, 0:2, :]).then_inc(s_half_read, 1)
                L.mark("half_read")

            def gates():
                dve.wait_ge(s_chunk_used, L.ended())
                dve.wait_ge(s_bias_in, 16)
                b = bfb[:].rearrange("p (a n) -> p a n", a=1).to_broadcast([P, TB, HEADS])
                tt(lf[:, 0], half()[:, 0:2, 0:HEADS], b).then_inc(s_half_read, 1)
                L.mark("half_read")
                dve.wait_ge(s_half_read, L.at("half_read"))
                V.tensor_scalar(lf[:, 4], lf[:, 0], 0.0, None, ALU.min).then_inc(s_dve_step, 1)
                L.mark("dve_step")
                L.add("gated")
                dve.wait_ge(s_gated, L.at("gated"))
                dve.wait_ge(s_dve_step, L.at("dve_step"))
                tt(lf[:, 5], lf[:, 4], lf[:, 3], ALU.subtract).then_inc(s_lf_ready, 1)
                L.mark("lf_ready", "lf")

            for branch in range(2):
                for g in range(4):
                    dst = (q2 if g < 2 else k2)[:, 4 * (g % 2):4 * (g % 2) + 4, :]
                    ahead(STD, lambda: halves_sum(dst, 4, HEAD_SCALE if g < 2 else 1.0))
                ahead(STD, lambda: values(0))
                if branch == 0:
                    ahead(STD, lambda: (values(1), second_attention("alibi", heads2[0])))
                else:
                    ahead(FG, lambda: values(1))
                    ahead(STD, lambda: (gates(), second_attention("fox", heads2[1])))

            def gate(side, i):
                L.add("gated")
                halves_sum(sigs[side][:, bass.ds(i * 4, 4), :])

            with L.loop(3) as i:
                ahead(STD, lambda: gate(0, i))
                ahead(STD, lambda: gate(1, i))
            ahead(STD, lambda: gate(0, 3))
            ahead(PRJ, lambda: gate(1, 3))

            def branch_a(i):
                halves_sum(conv_y[0])
                dve.wait_ge(s_half_read, L.at("half_read"))
                dve.wait_ge(s_gated, L.at("gated"))
                tt(conv_y[0], conv_y[0], sigs[0][:, bass.ds(i * 4, 4), :], ALU.mult).then_inc(s_dve_step, 1)
                L.mark("dve_step")

            def branch_b(i, key=None):
                halves_sum(conv_y[1])
                dve.wait_ge(s_half_read, L.at("half_read"))
                tt(conv_y[1], conv_y[1], sigs[1][:, bass.ds(i * 4, 4), :], ALU.mult).then_inc(s_dve_step, 1)
                L.mark("dve_step")
                dve.wait_ge(s_dve_step, L.at("dve_step"))
                tt(conv_y[1], conv_y[1], conv_y[0]).then_inc(s_batch, 1)
                L.mark("batch")
                dve.wait_ge(s_batch, L.at("batch"))
                lo_batch(h2, i * 4, 4, key)

            with L.loop(3) as i:
                ahead(PRJ, lambda: branch_a(i))
                ahead(PRJ, lambda: branch_b(i))
            ahead(PRJ, lambda: branch_a(3))
            ahead(STD, lambda: branch_b(3, "merged"))

            def norm_hm():
                dve.wait_ge(s_half_read, L.at("half_read"))
                square_count(4)
                inverse(T)
                norm("hm", KT, xt, lambda k: col("norm_mlp_g_2", k), hf)

            for g in range(4):
                ahead(STD, lambda: (onto_x(4 * g), norm_hm() if g == 3 else None))

            def squared_relu(buf, t, key=None):
                halves_sum(conv_y[0])
                dve.wait_ge(s_half_read, L.at("half_read"))
                V.scalar_tensor_tensor(conv_y[1], conv_y[0], 0.0, conv_y[0], ALU.max, ALU.mult).then_inc(s_batch, 1)
                L.mark("batch")
                dve.wait_ge(s_batch, L.at("batch"))
                lo_batch(hid[buf], t, 4, key)

            for f in range(5):
                if f < 4:
                    with L.loop(2) as i:
                        for g in range(2):
                            ahead(STD, lambda: squared_relu(f % 2, i * 8 + 4 * g, ("hid2", f) if g else None))
                if 0 < f < 4:
                    with L.loop(2) as i:
                        for g in range(2):
                            ahead(STD, lambda: onto_x(i * 8 + 4 * g))
            for g in range(3):
                ahead(STD, lambda: onto_x(4 * g))
            L.end = L.n["hi_ready"]
            onto_x(12)
            norm_onto_x("norm_final_g_2")
            for tb in range(TB):
                dve.wait_ge(s_turned, L.of("turned", ("out", tb)))
                V.tensor_copy(outrow[:, tb, :], half()[:].rearrange("p b n -> p (b n)")).then_inc(s_half_read, 1)
                L.mark("half_read", ("row", tb))

        @block.tensor
        def _(pe):
            L = Stream(pe, "pe", known, traced)
            mm = nc.tensor.matmul

            def half(ahead_=0):
                return halves[(L.n.get("half_read", 0) + ahead_) % 2]

            def free(turns=1):
                if L.n.get("half_read", 0) + turns > 2:
                    pe.wait_ge(s_half_read, L.at("half_read", turns - 2))

            def turn(k=1):
                L.add("half_read", k)

            def chunk(width):
                L.add("drained")
                pe.wait_ge(s_drained, L.at("drained"))
                s = L.split_slot()
                return [w[:, s, :] for w in (whi, wlo)]

            def tiles(nk, width, ready=None):
                for k0 in range(0, nk, KC):
                    if ready:
                        pe.wait_ge(s_act_lo, L.of("act_lo", (ready, min(k0 + KC, nk) - 1)))
                    hi, lo = chunk(width)
                    n = min(KC, nk - k0)
                    for k in range(n):
                        at = slice(k * width, (k + 1) * width)
                        yield k0 + k, hi[:, at], lo[:, at], k == n - 1

            def product(operands, nk=KT, width=GW, blocks=(0, P, 2 * P, 3 * P), ready=None, k_at=0):
                free(len(operands))
                for k, hi, lo, last in tiles(nk, width, ready):
                    for a, (src, nth) in enumerate(operands):
                        for b, at in enumerate(blocks):
                            o = half(nth)[:, b, :]
                            mm(o, hi[:, at:at + P], src(k_at + k), start=(k == 0), stop=False)
                            ins_ = mm(o[:, 0:T], lo[:, at:at + P], src(k_at + k)[:, 0:T], start=False, stop=(k == nk - 1))
                    if last:
                        ins_.then_inc(s_chunk_used, 1)
                        L.mark("chunk_used")
                        L.add("hi_ready")
                turn(len(operands))

            def of(t, k0=0):
                return [(lambda k: t[:, k0 + k, :], 0)]

            def token_product(t, width=GW, ready=None, nk=KT):
                free()
                for k, hi, lo, last in tiles(nk, width, ready):
                    for tb in range(TB):
                        o = half()[:, tb, 0:width]
                        xh, xl = t[:, k, tb * P:(tb + 1) * P], t[:, k, T + tb * P:T + (tb + 1) * P]
                        mm(o, xh, hi, start=(k == 0), stop=False)
                        mm(o, xh, lo, start=False, stop=False)
                        ins_ = mm(o, xl, hi, start=False, stop=(k == nk - 1))
                    if last:
                        ins_.then_inc(s_chunk_used, 1)
                        L.mark("chunk_used")
                        L.add("hi_ready")
                turn()

            def groups(n, t, k0=0, nk=KT, ready=None):
                with L.loop(n // 2):
                    product(of(t, k0), nk, ready=ready)
                    product(of(t, k0), nk, ready=ready)

            def mod():
                L.add("drained", GC)
                pe.wait_ge(s_drained, L.at("drained"))
                free()
                slot = L.n.get("mod_summed", 0) % 2
                for b in range(4):
                    ins_ = mm(half()[:, 0, b:b + 1], acc[:, slot, b * P:(b + 1) * P], ones[:, 0:1], start=True, stop=True)
                ins_.then_inc(s_mod_summed, 1)
                L.mark("mod_summed")
                turn()

            def sums(chunks=4, width=T, n=None):
                free()
                per = 4 * T // width
                for c in range(chunks):
                    j = L.n.get("squared", 0)
                    pe.wait_ge(s_squared, L.of("squared", j))
                    for b in range(per):
                        ins_ = mm(half()[:, 0, 0:width], ones[:], sq[:, j % 2, b * width:(b + 1) * width],
                                  start=(c + b == 0), stop=(c == chunks - 1 and b == per - 1))
                    ins_.then_inc(s_summed, 1)
                    L.mark("summed", ("sq", j))
                    L.add("squared")
                turn()

            pe.wait_ge(s_const_in, 32)
            pe.wait_ge(s_vec_in, 16 * len(VEC_AT))
            for g, n in enumerate(VEC_ROWS):
                ins_ = nc.tensor.transpose(half()[:, g // 3, (g % 3) * P:(g % 3) * P + n], vrows[0:n, g, :], ident[0:n, 0:n])
            ins_.then_inc(s_turned, 1)
            L.mark("turned", "vec")
            turn()
            pe.wait_ge(s_x_in, 64)
            for tb in range(4):
                free()
                for k in range(KT):
                    ins_ = nc.tensor.transpose(half()[:, k // 4, (k % 4) * P:(k % 4 + 1) * P],
                                               stage[:, tb, k * P:(k + 1) * P], ident[:])
                ins_.then_inc(s_turned, 1)
                L.mark("turned", tb)
                turn()
            pe.wait_ge(s_filled, L.of("filled", "ones"))
            pe.wait_ge(s_cst_ready, L.of("cst_ready", "lo"))

            def rows():
                free()
                for k, hi, lo, last in tiles(KT, GW):
                    mm(half()[:, 0, :], cst[:, k, :], hi, start=(k == 0), stop=False)
                    ins_ = mm(half()[:, 0, :], cst[:, k, :], lo, start=False, stop=(k == KT - 1))
                    if last:
                        ins_.then_inc(s_chunk_used, 1)
                        L.mark("chunk_used")
                        L.add("hi_ready")
                s = L.n.get("row_ready", 0) % 2
                L.add("row_ready")
                pe.wait_ge(s_row_ready, L.at("row_ready"))
                for b in range(4):
                    ins_ = mm(half()[:, 1, 2 * b:2 * b + 2], row4[0:4, s, b * P:(b + 1) * P], sel[0:4, :], start=True, stop=True)
                ins_.then_inc(s_row_summed, 1)
                L.mark("row_summed")
                turn()

            with L.loop(4):
                rows()
                rows()
            sums()
            sums()
            pe.wait_ge(s_act_lo, L.of("act_lo", ("hctx", KT - 1)))
            product([(lambda k: h1[:, k, :], 0), (lambda k: hctx[:, k, :], 1)], width=KVR + ROPE, blocks=(0, P, KVR + ROPE - P))
            product(of(h1))
            mod()
            with L.loop(3):
                for _ in range(2):
                    product(of(h1))
                    mod()
            sums(1)
            sums(1, 2 * T)
            pe.wait_ge(s_act_lo, L.of("act_lo", ("qn", 3)))
            with L.loop(2):
                for _ in range(2):
                    product(of(qn), 4, 384, (0, ROPE, 192, 192 + ROPE))
            mod()
            pe.wait_ge(s_act_lo, L.of("act_lo", ("kvn", 1)))
            for g in range(4):
                free(2)
                for k, hi, lo, last in tiles(KC, GW):
                    for b in range(4):
                        o, at, x = half()[:, b, :], (b // 2) * 2 * P, kvn[:, k, (b % 2) * 2 * T:(b % 2 + 1) * 2 * T]
                        mm(o, hi[:, at:at + P], x, start=(k == 0), stop=False)
                        mm(o[:, 0:T], lo[:, at:at + P], x[:, 0:T], start=False, stop=(k == KC - 1))
                parts = [(k, hi2, lo2) for k, hi2, lo2 in
                         [(k, whi[:, L.split_slot(), k * GW:(k + 1) * GW], wlo[:, L.split_slot(), k * GW:(k + 1) * GW]) for k in range(KC)]]
                for s in range(4):
                    o = half(1)[:, s // 2, (s % 2) * 2 * P:(s % 2 + 1) * 2 * P].rearrange("p (h n) -> p h n", h=2)
                    for k, hi, lo in parts:
                        vh, vl = [w.rearrange("p (h a n) -> p h a n", h=2, a=2)[:, :, 1, :] for w in (hi, lo)]
                        base = (s // 2) * 2 * T + (s % 2) * P
                        xh, xl = kvn[:, k, base:base + P], kvn[:, k, base + T:base + T + P]
                        mm(o, xh, vh, start=(k == 0), stop=False)
                        mm(o, xh, vl, start=False, stop=False)
                        ins_ = mm(o, xl, vh, start=False, stop=(k == KC - 1))
                ins_.then_inc(s_chunk_used, 1)
                L.mark("chunk_used")
                L.add("hi_ready")
                turn(2)
            pe.wait_ge(s_rope_in, 32)
            free()
            pe.wait_ge(s_half_read, L.of("half_read", ("q", 3)))
            for b in range(4):
                ins_ = mm(half()[ROPE:P, b, :], swap[ROPE:P, :], qrt[ROPE:P, 2 * b:2 * b + 2, :].rearrange("p h t -> p (h t)"),
                          start=True, stop=True)
            ins_.then_inc(s_projected, 1)
            L.mark("projected", "q")
            turn()
            free()
            mm(half()[ROPE:P, 0, 0:T], swap[ROPE:P, :], krope[ROPE:P, 0:T], start=True, stop=True)\
                .then_inc(s_projected, 1)
            L.mark("projected", "k")
            turn()

            def attention(tag, score, turn_p, weighted):
                free(2)
                for h in range(HEADS + 1):
                    if h < HEADS:
                        for qb in range(TB):
                            score(h, qb, bank(2 * (h % 2) + qb)).then_inc(s_scores, 1)
                            L.mark("scores", (tag, h, qb))
                    if h > 0:
                        g = h - 1
                        for qb in range(TB):
                            pe.wait_ge(s_probs, L.of("probs", (tag, g, qb)))
                            ins_ = turn_p(g, qb)
                        ins_.then_inc(s_pt_turned, 1)
                        L.mark("pt_turned", (tag, g))
                        pe.wait_ge(s_pt_copied, L.of("pt_copied", (tag, g)))
                        if g >= 2 and tag == "mla":
                            pe.wait_ge(s_heads_read, L.of("heads_read", (tag, g - 2)))
                        elif g >= 2:
                            pe.wait_ge(s_act_lo, L.of("act_lo", (tag, g - 2)))
                        weighted(g, bank(6 + g % 2)).then_inc(s_heads, 1)
                        L.mark("heads", (tag, g))
                turn(2)

            def score1(h, qb, o):
                mm(o, qt[:, h, qb * P:(qb + 1) * P], ktt[:, h, :], start=True, stop=False)
                return mm(o, qrt[ROPE:P, h, qb * P:(qb + 1) * P], krope[ROPE:P, :], start=False, stop=True)

            def turn1(h, qb):
                for kb in range(4):
                    at = (kb % 2) * T + qb * P
                    ins_ = nc.tensor.transpose(bank(4 + kb // 2)[:, at:at + P], pr1[:, h % 2, qb, kb * P:(kb + 1) * P], ident[:])
                return ins_

            def weighted1(h, o):
                for kb in range(4):
                    ins_ = mm(o[:, 0:T], vt[:, kb, h * P:(h + 1) * P], pt1[:, h % 2, kb, :], start=(kb == 0), stop=(kb == 3))
                return ins_

            pe.wait_ge(s_stored_x, L.of("stored_x", "krope"))
            attention("mla", score1, turn1, weighted1)
            pe.wait_ge(s_half_read, L.of("half_read", "mla done"))
            for j in range(4):
                n = L.n["squared"]
                pe.wait_ge(s_squared, L.of("squared", n))
                for b in range(2):
                    ins_ = mm(half(j // 2)[:, 2 * (j % 2) + b, :], ones[:], sq[:, n % 2, b * 2 * T:(b + 1) * 2 * T],
                              start=True, stop=True)
                ins_.then_inc(s_summed, 1)
                L.mark("summed", ("sq", n))
                L.add("squared")
            turn(2)
            with L.loop(2):
                for _ in range(2):
                    product(of(mix), ready="mix")
                    mod()
            sums()
            with L.loop(2):
                for _ in range(2):
                    product(of(hf), ready="hf")
                    product(of(hf))
                mod()
                mod()
            groups(8, hf)
            pe.wait_ge(s_act_lo, L.of("act_lo", ("hid", 0)))
            groups(4, hid[0])
            with L.loop(2):
                product(of(hf))
                product(of(hf))
            product(of(hf), width=3 * P, blocks=(0, P, 2 * P))
            product(of(hf), width=3 * P, blocks=(0, P, 2 * P))
            pe.wait_ge(s_act_lo, L.of("act_lo", ("hid", 1)))
            groups(4, hid[1])
            pe.wait_ge(s_act_lo, L.of("act_lo", ("hid", 2)))
            for g in range(4):
                product(of(hid[0]), FT - 2 * HT)
            sums()
            sums()

            def score2(tag):
                def score(h, qb, o):
                    nk = (qb + 1) * P
                    ins_ = mm(o[:, 0:nk], q2[:, h, qb * P:(qb + 1) * P], k2[:, h, 0:nk], start=True, stop=(tag == "alibi"))
                    if tag == "fox":
                        for s in range(qb + 1):
                            pe.wait_ge(s_lfw, L.of("lfw", (h, s)))
                            ins_ = mm(o[:, 0:nk], lfw[:, h % 2, s, qb * P:(qb + 1) * P], after[:, s, 0:nk], start=False, stop=(s == qb))
                    return ins_
                return score

            def turn2(h, qb):
                for kb in range(qb + 1):
                    at = qb * P if kb == 0 else 2 * P
                    ins_ = nc.tensor.transpose(bank(4)[:, at:at + P], p2[:, h % 2, qb, kb * P:(kb + 1) * P], ident[:])
                return ins_

            def weighted2(h, o):
                pt = pt2[:, h % 2, :, :].rearrange("p a t -> p (a t)")
                mm(o[:, 0:T], v2[:, 0, h * P:(h + 1) * P], pt[:, 0:T], start=True, stop=False)
                return mm(o[:, P:T], v2[:, 1, h * P:(h + 1) * P], pt[:, T:T + P], start=False, stop=True)

            for branch, tag in enumerate(("alibi", "fox")):
                with L.loop(2):
                    for _ in range(2):
                        product(of(h2), ready="h2" if branch == 0 else None)
                token_product(h2)
                token_product(h2)
                if tag == "fox":
                    free()
                    hi, lo = chunk(8)
                    for k in range(KT):
                        at = slice(8 * k, 8 * k + 8)
                        for tb in range(TB):
                            o, xh, xl = half()[:, tb, 0:8], h2[:, k, tb * P:(tb + 1) * P], h2[:, k, T + tb * P:T + (tb + 1) * P]
                            mm(o, xh, hi[:, at], start=(k == 0), stop=False)
                            mm(o, xh, lo[:, at], start=False, stop=False)
                            ins_ = mm(o, xl, hi[:, at], start=False, stop=(k == KT - 1))
                    ins_.then_inc(s_chunk_used, 1)
                    L.mark("chunk_used")
                    L.add("hi_ready")
                    turn()
                    pe.wait_ge(s_mask_in, 64)
                free(2)
                attention(tag, score2(tag), turn2, weighted2)
                pe.wait_ge(s_half_read, L.of("half_read", (tag, "done")))
            with L.loop(4):
                product(of(h2))
                product(of(h2))
            with L.loop(4):
                product(of(heads2[0]), 8)
                product(of(heads2[1]), 8)
            pe.wait_ge(s_act_lo, L.of("act_lo", "merged"))
            groups(4, h2)
            sums()
            for f in range(5):
                if f < 4:
                    groups(4, hf, ready="hm" if f == 0 else None)
                if f > 0:
                    pe.wait_ge(s_act_lo, L.of("act_lo", ("hid2", f - 1)))
                    groups(4, hid[(f - 1) % 2])
            sums()
            pe.wait_ge(s_stored_x, L.of("stored_x", "norm_final_g_2"))
            for tb in range(TB):
                free()
                for k in range(KT):
                    ins_ = nc.tensor.transpose(half()[:, k // 4, (k % 4) * P:(k % 4 + 1) * P],
                                               xt[:, k, tb * P:(tb + 1) * P], ident[:])
                ins_.then_inc(s_turned, 1)
                L.mark("turned", ("out", tb))
                turn()


INPUTS = ["x", "c", "ctx", "c_ctx", "w_ada", "b_ada", "g_mix_norm", "w_in", "g_q_a", "w_q_b", "g_kv_a", "w_kv_b",
          "conv_w", "conv_b", "g_mix_out", "w_out", "g_ffn_norm", "w_up", "ffn_conv_w", "ffn_conv_b", "w_down",
          "g_final", "norm_mix_g_2", "w_in_2", "b_forget_2", "w_proj_a_2", "w_proj_b_2", "w_out_2", "norm_mlp_g_2",
          "w_up_2", "w_down_2", "norm_final_g_2"]


def kernel(**inputs):
    import concourse.bacc as bacc
    from concourse.bass_utils import run_bass_kernel_spmd

    arrays = {f"in_{n}": np.ascontiguousarray(inputs[n]) for n in INPUTS}
    tables = {f"table_{n}": a for n, a in constants().items()}

    def trace(known):
        nc = bacc.Bacc("TRN2", target_bir_lowering=False, num_devices=1)
        ins = {n: nc.dram_tensor(f"in_{n}", arrays[f"in_{n}"].shape, F32, kind="ExternalInput").ap() for n in INPUTS}
        consts = {n[6:]: nc.dram_tensor(n, a.shape, F32, kind="ExternalInput").ap() for n, a in tables.items()}
        out = nc.dram_tensor("out", (1, T, D), F32, kind="ExternalOutput").ap()
        traced = {}
        program(nc, ins, consts, out, known, traced)
        return nc, traced

    known = {}
    for _ in range(3):
        nc, traced = trace(known)
        known, before = traced, known
    assert known == before
    r = run_bass_kernel_spmd(nc, [{**arrays, **tables}], core_ids=[0])
    return r.results[0]["out"]
```

```python
from contextlib import ExitStack, contextmanager

import numpy as np

import concourse.bass as bass
from concourse import mybir

P = 128
D = 2048
T = 256
KT = D // P
TB = T // P
GW = 512
KC = 2
CW = KC * GW
GC = KT // KC
NRAW = 8
NSPLIT = 4
NACC = 4
HEADS = 8
QR, KVR, ROPE = 512, 256, 64
FFN = 5504
FT = FFN // P
FF2 = 8192
HT = 16
EPS = 1e-6
MLA_SCALE = float((128 + 64) ** -0.5)
HEAD_SCALE = float(128 ** -0.5)
FAR = 1.0e30

F32 = mybir.dt.float32
F32R = mybir.dt.float32r
ACT = mybir.ActivationFunctionType
ALU = mybir.AluOpType
AX = mybir.AxisListType.X

VEC_GROUPS = [
    [("c", 16), ("c_ctx", 16), ("b_ada", 96)],
    [("g_mix_norm", 16), ("g_q_a", 4), ("g_kv_a", 2), ("conv_w", 24), ("conv_b", 8), ("g_mix_out", 16),
     ("g_ffn_norm", 16), ("g_final", 16), ("norm_mix_g_2", 16)],
    [("norm_mlp_g_2", 16), ("norm_final_g_2", 16), ("ffn_conv_b", 86)],
    [("ffn_conv_w0", 86)], [("ffn_conv_w1", 86)], [("ffn_conv_w2", 86)],
]
VEC_AT = {}
for _g, _names in enumerate(VEC_GROUPS):
    _r = 0
    for _name, _n in _names:
        VEC_AT[_name] = (_g, _r, _n)
        _r += _n
VEC_ROWS = [sum(n for _, n in names) for names in VEC_GROUPS]


def constants():
    c = {"ident": np.eye(P, dtype=np.float32)}
    sel = np.zeros((4, 2), np.float32)
    sel[[0, 2], 0] = 1
    sel[[1, 3], 1] = 1
    c["sel"] = sel
    t = np.arange(T)
    inv = (np.float32(10000.0) ** (-np.arange(0, 32, 2, dtype=np.float32) / np.float32(32))).astype(np.float32)
    row, col = (t // 64).astype(np.float32), (t % 64).astype(np.float32)
    ang = np.concatenate([row[:, None] * inv, col[:, None] * inv], axis=-1)
    cos, sin = np.cos(ang).astype(np.float32), np.sin(ang).astype(np.float32)
    d = np.arange(ROPE)
    sign = np.where(d % 2 == 0, -1.0, 1.0).astype(np.float32)
    c["rope"] = np.stack([cos[:, d // 2].T, sin[:, d // 2].T * sign[:, None]], 1).astype(np.float32).reshape(ROPE, 2 * T)
    swap = np.zeros((ROPE, ROPE), np.float32)
    swap[d, d ^ 1] = 1
    c["swap"] = swap
    q, k = np.arange(T)[:, None], np.arange(T)[None, :]
    blocks = lambda a: a.reshape(TB, P, T).transpose(1, 0, 2).reshape(P, TB * T).astype(np.float32)
    c["dist"] = blocks(np.where(q >= k, q - k, FAR))
    c["causal"] = blocks(np.where(q >= k, 0.0, -FAR))
    c["upto"] = blocks(q <= k)
    c["after"] = blocks(q > k)
    return {n: np.ascontiguousarray(a, np.float32) for n, a in c.items()}


class Ledger:

    def __init__(self, eng, name, known, traced):
        self.eng, self.name, self.known, self.traced = eng, name, known, traced
        self.n, self.loops, self.reg, self.per, self.trips = {}, 0, None, {}, 1

    def at(self, what, extra=0):
        base = self.n.get(what, 0) + extra
        return base + self.reg * self.per[what] if self.reg is not None and self.per.get(what) else base

    def add(self, what, k=1):
        self.n[what] = self.n.get(what, 0) + k

    def mark(self, sem, key=None):
        self.add(sem)
        if key is not None:
            assert (sem, key) not in self.traced, (sem, key)
            self.traced[sem, key] = (self.n[sem], self.per.get(sem, 0), self.trips if self.reg is not None else 1)

    def of(self, sem, key):
        value, per, trips = self.known.get((sem, key), (1, 0, 1))
        if self.reg is not None and self.trips == trips and per:
            return self.reg * per + value
        return value + per * (trips - 1)

    @contextmanager
    def loop(self, trips):
        start, me = dict(self.n), (self.name, self.loops)
        self.loops += 1
        self.per, self.trips = self.known.get(me, {}), trips
        with self.eng.Fori(0, trips) as i:
            self.reg = i
            yield i
        ring, slots = ("hi_ready", NSPLIT) if self.name == "pe" else ("drained", NRAW)
        assert self.name != "pe" or (self.n.get("mod_summed", 0) - start.get("mod_summed", 0)) % NACC == 0
        assert (self.n.get(ring, 0) - start.get(ring, 0)) % slots == 0
        assert self.n.get("half_read", 0) % 2 == start.get("half_read", 0) % 2
        self.reg = None
        moved = {k: v - start.get(k, 0) for k, v in self.n.items() if v != start.get(k, 0)}
        self.traced[me] = moved
        for k, v in moved.items():
            self.n[k] = start.get(k, 0) + trips * v


class Stream(Ledger):

    end = 0
    mod_open = False

    def ended(self):
        per = self.per.get("hi_ready", 0) if self.reg is not None else 0
        return self.reg * per + self.end if per else self.end

    def raw_slot(self):
        return self.n.get("drained", 0) % NRAW

    def split_slot(self):
        return self.n.get("hi_ready", 0) % NSPLIT

    def loads(self):
        c = self.n.get("drained", 0)
        per = self.per.get("drained", 0) * 16 // NRAW if self.reg is not None else 0
        value = 16 * (c // NRAW + 1)
        return self.reg * per + value if per else value


STD = (CW,) * GC
KVG = (KC * (KVR + ROPE),) * GC
QBG = (KC * 384,) * 2
KVB = (CW,)
TAIL = (KC * 384,) * GC
DN11 = (CW,) * 5 + (GW,)
FG = (KT * 8,)
PRJ = (CW,) * 4
CONV_COLS = [at + GW * i for i in range(2) for at in (1856, 2880, 832)]
F_AT, GA_AT, GB_AT = 6144, 6152, 8200


def program(nc, ins, consts, out, known, traced):
    with ExitStack() as ctx:
        def sb(name, shape, dt=F32, scope=ctx):
            return scope.enter_context(nc.sbuf_tensor(name, shape, dt))

        raw_in = [ctx.enter_context(nc.semaphore(f"raw_in{i}")) for i in range(NRAW)]
        def sem(name):
            return ctx.enter_context(nc.semaphore(name))

        s_hi_ready = sem("hi_ready")
        s_drained = sem("drained")
        s_chunk_used = sem("chunk_used")
        s_half_read = sem("half_read")
        s_const_in = sem("const_in")
        s_vec_in = sem("vec_in")
        s_x_in = sem("x_in")
        s_rope_in = sem("rope_in")
        s_mask_in = sem("mask_in")
        s_bias_in = sem("bias_in")
        s_stored = sem("stored")
        s_filled = sem("filled")
        s_act_step = sem("act_step")
        s_dve_step = sem("dve_step")
        s_turned = sem("turned")
        s_summed = sem("summed")
        s_projected = sem("projected")
        s_silu = sem("silu")
        s_copied = sem("copied")
        s_squared = sem("squared")
        s_root = sem("root")
        s_rounded = sem("rounded")
        s_rounded_batch = sem("rounded_batch")
        s_tapped = sem("tapped")
        s_gated = sem("gated")
        s_columns = sem("columns")
        s_cst_ready = sem("cst_ready")
        s_row_ready = sem("row_ready")
        s_row_summed = sem("row_summed")
        s_mod_read = sem("mod_read")
        s_mod_summed = sem("mod_summed")
        s_conved = sem("conved")
        s_batch = sem("batch")
        s_normed = sem("normed")
        s_act_lo = sem("act_lo")
        s_padded = sem("padded")
        s_stored_x = sem("stored_x")
        s_scores = sem("scores")
        s_maxed = sem("maxed")
        s_expd = sem("expd")
        s_probs = sem("probs")
        s_pt_turned = sem("pt_turned")
        s_pt_copied = sem("pt_copied")
        s_heads = sem("heads")
        s_heads_read = sem("heads_read")
        s_lf_ready = sem("lf_ready")
        s_lfw = sem("lfw")

        halves = [ctx.enter_context(nc.psum_tensor(f"half{i}", [P, 4, 512], F32)) for i in range(2)]

        def bank(i):
            return halves[i // 4][:, i % 4, :]

        xt = sb("xt", [P, KT, T])
        raw = sb("raw", [P, NRAW, CW])
        whi = sb("whi", [P, NSPLIT, CW], F32R)
        wlo = sb("wlo", [P, NSPLIT, CW], F32R)
        vec = sb("vec", [P, 6, P])
        ident = sb("ident_sb", [P, P])
        ones = sb("ones", [P, P])
        sel = sb("sel_sb", [4, 2])
        rstd = sb("rstd", [P, 2 * T])
        sq = sb("sq", [P, 2, 4 * T])
        tmp = sb("tmp", [P, 4, T])
        zpad = sb("zpad", [P, 4, T + 2])
        mod_a = sb("mod_a", [P, 32, 2])
        mod_f = sb("mod_f", [P, 64])
        gain = sb("gain", [P, KT, 3])
        silu = sb("silu_sb", [P, 32])
        stat = sb("stat", [P, 64])
        lf = sb("lf", [P, 6, TB, HEADS])
        bfb = sb("bfb", [P, HEADS])
        eps = sb("eps", [P, 1])

        first = ExitStack()
        t16 = sb("t16", [P, KT, T], scope=first)
        krope = sb("krope", [P, 2 * T], scope=first)
        acc = sb("acc", [P, NACC, GW], scope=first)
        sc = ExitStack()
        stage = sb("stage", [P, 4, D], scope=sc)
        cst = sb("cst", [P, KT, P], F32R, scope=sc)
        vrows = sb("vrows", [P, 6, P], scope=sc)
        row4 = sb("row4", [4, 2, GW], scope=sc)
        sc.close()
        sc = ExitStack()
        h1 = sb("h1", [P, KT, 2 * T], F32R, scope=sc)
        sc2 = ExitStack()
        hctx = sb("hctx", [P, KT, 2 * T], F32R, scope=sc2)
        sc2.close()
        sc2 = ExitStack()
        qraw = sb("qraw", [P, 4, T], scope=sc2)
        kvraw = sb("kvraw", [P, 2, 2 * T], scope=sc2)
        sc2.close()
        sc.close()
        sc = ExitStack()
        rope = sb("rope_sb", [P, 2, T], scope=sc)
        swap = sb("swap_sb", [P, ROPE], scope=sc)
        qt = sb("qt", [P, HEADS, T], scope=sc)
        qrt = sb("qrt", [P, HEADS, T], scope=sc)
        ktt = sb("ktt", [P, HEADS, 2 * T], scope=sc)
        vt = sb("vt", [P, 4, HEADS * P], scope=sc)
        sc2 = ExitStack()
        qn = sb("qn", [P, 4, 2 * T], F32R, scope=sc2)
        kvn = sb("kvn", [P, 2, 4 * T], F32R, scope=sc2)
        sc2.close()
        sc2 = ExitStack()
        pr1 = sb("pr1", [P, 2, 2, 2 * T], scope=sc2)
        pt1 = sb("pt1", [P, 2, 4, T], scope=sc2)
        sc2.close()
        sc.close()
        sc = ExitStack()
        mix = sb("mix", [P, KT, 2 * T], F32R, scope=sc)
        sc.close()
        first.close()

        sc = ExitStack()
        hf = sb("hf", [P, KT, 2 * T], F32R, scope=sc)
        hid = [sb(f"hid{i}", [P, HT, 2 * T], F32R, scope=sc) for i in range(2)]
        sc.close()

        sc = ExitStack()
        heads2 = [sb(f"heads2_{i}", [P, HEADS, 2 * T], F32R, scope=sc) for i in range(2)]
        h2 = sb("h2", [P, KT, 2 * T], F32R, scope=sc)
        sc2 = ExitStack()
        q2 = sb("q2", [P, HEADS, T], scope=sc2)
        k2 = sb("k2", [P, HEADS, T], scope=sc2)
        v2 = sb("v2", [P, TB, HEADS * P], scope=sc2)
        dist = sb("dist_sb", [P, TB, T], scope=sc2)
        causal = sb("causal_sb", [P, TB, T], scope=sc2)
        upto = sb("upto_sb", [P, TB, T], scope=sc2)
        after = sb("after_sb", [P, TB, T], scope=sc2)
        sc2.close()
        sc2 = ExitStack()
        sigs = [sb(f"sig{i}", [P, KT, T], scope=sc2) for i in range(2)]
        sc2.close()
        sc.close()
        sc = ExitStack()
        outrow = sb("outrow", [P, TB, D], scope=sc)
        sc.close()

        p2 = sq[:, 0, :].rearrange("p (a b t) -> p a b t", a=2, b=2)
        pt2 = sq[:, 1, :].rearrange("p (a b t) -> p a b t", a=2, b=2)
        lfw = tmp[:, :, :].rearrange("p (a b) t -> p a b t", a=2)
        conv_y = [sq[:, i, :].rearrange("p (b t) -> p b t", b=4) for i in range(2)]

        def col(name, i=0):
            g, r, _ = VEC_AT[name]
            return vec[:, g, bass.ds(i + r, 1)]

        def cols(name, i, n):
            g, r, _ = VEC_AT[name]
            return vec[:, g, bass.ds(i + r, n)]

        W = {n: ins[n][0].rearrange("(k p) n -> p k n", p=P)
             for n in ("w_ada", "w_in", "w_q_b", "w_kv_b", "w_out", "w_up", "w_down")}
        W.update({n: ins[n].rearrange("(k p) n -> p k n", p=P)
                  for n in ("w_in_2", "w_proj_a_2", "w_proj_b_2", "w_out_2", "w_up_2", "w_down_2")})
        flat = lambda t: t[:].rearrange("p k t -> p (k t)")
        block = ctx.enter_context(nc.Block())

        @block.sync
        def _(sp):
            L = Stream(sp, "sp", known, traced)

            def load(w, k0, nk, c0, width):
                if L.n.get("drained", 0) >= NRAW:
                    sp.wait_ge(s_drained, L.at("drained", 1 - NRAW))
                dst = raw[:, L.raw_slot(), 0:nk * width].rearrange("p (k n) -> p k n", k=nk)
                sp.dma_start(dst, w[:, k0:k0 + nk, bass.ds(c0, width)]).then_inc(raw_in[L.raw_slot()], 16)
                L.add("drained")

            def group(name, c0, width=GW, k0=0, nk=KT):
                for k in range(k0, k0 + nk, KC):
                    load(W[name], k, min(KC, k0 + nk - k), c0, width)

            def with_sum(name, c0, width=GW):
                for k in range(0, KT, KC):
                    load(W[name], k, KC, c0, width)
                    load_mod(1)

            def load_mod(chunks):
                for _ in range(chunks):
                    n = L.n.get("mod_chunks", 0)
                    load(W["w_ada"], KC * (n % GC), KC, (8 + n // GC) * GW, GW)
                    L.add("mod_chunks")

            def groups(name, n, base=0, k0=0, nk=KT):
                with L.loop(n // 2) as i:
                    for g in range(2):
                        group(name, i * (2 * GW) + (base + g * GW), GW, k0, nk)

            sp.dma_start(ident[:], consts["ident"]).then_inc(s_const_in, 16)
            sp.dma_start(sel[:], consts["sel"]).then_inc(s_const_in, 16)
            for tb in range(TB):
                sp.dma_start(stage[:, tb, :], ins["x"][0, tb * P:(tb + 1) * P, :]).then_inc(s_x_in, 16)
            group("w_ada", 0)
            group("w_ada", GW)
            groups("w_ada", 6, 2 * GW)
            with_sum("w_in", QR, KVR + ROPE)
            with_sum("w_in", 0)
            for at in CONV_COLS:
                with_sum("w_in", at)
            for g in range(4):
                group("w_q_b", g * 384, 384, 0, 4)
            for g in range(4):
                group("w_kv_b", g * GW, GW, 0, KC)
                load_mod(2)
            sp.wait_ge(s_act_lo, L.of("act_lo", ("kvn", 1)))
            sp.dma_start(rope[ROPE:P, :, :], consts["rope"].rearrange("p (a t) -> p a t", a=2)).then_inc(s_rope_in, 16)
            sp.dma_start(swap[ROPE:P, :], consts["swap"]).then_inc(s_rope_in, 16)
            group("w_out", 0, GW, 0, KT // 2)
            load_mod(4 * HEADS)
            group("w_out", 0, GW, KT // 2, KT // 2)
            for g in range(1, 4):
                with_sum("w_out", g * GW)
            with L.loop(2) as i:
                for g in range(2):
                    group("w_up", i * (2 * GW) + g * GW)
                    group("w_up", i * (2 * GW) + (g * GW + FFN))

            def pairs(tile, n):
                with L.loop(n) as i:
                    group("w_up", i * GW + tile * P)
                    group("w_up", i * GW + (FFN + tile * P))

            pairs(HT, 4)
            groups("w_down", 4)
            pairs(2 * HT, 2)
            group("w_up", 40 * P, 3 * P)
            group("w_up", FFN + 40 * P, 3 * P)
            groups("w_down", 4, 0, HT)
            for g in range(4):
                group("w_down", g * GW, GW, 2 * HT, FT - 2 * HT)
            groups("w_in_2", 6)
            sp.wait_ge(s_act_lo, L.of("act_lo", ("h2", KT - 1)))
            for t, n in ((dist, "dist"), (causal, "causal"), (upto, "upto"), (after, "after")):
                sp.dma_start(t[:], consts[n].rearrange("p (a t) -> p a t", a=TB)).then_inc(s_mask_in, 16)
            groups("w_in_2", 6, 3072)
            load(W["w_in_2"], 0, KT, F_AT, 8)
            with L.loop(4) as i:
                group("w_in_2", i * GW + GA_AT)
                group("w_in_2", i * GW + GB_AT)
            with L.loop(4) as i:
                group("w_proj_a_2", i * GW, GW, 0, 8)
                group("w_proj_b_2", i * GW, GW, 0, 8)
            groups("w_out_2", 4)
            for f in range(5):
                if f < 4:
                    groups("w_up_2", 4, f * D)
                if f > 0:
                    groups("w_down_2", 4, 0, (f - 1) * HT)
            for tb in range(TB):
                sp.wait_ge(s_half_read, L.of("half_read", ("row", tb)))
                sp.dma_start(out[0, tb * P:(tb + 1) * P, :], outrow[:, tb, :]).then_inc(s_stored, 16)
            sp.wait_ge(s_stored, 16 * TB)

        @block.gpsimd
        def _(pool):
            L = Stream(pool, "pool", known, traced)
            nc.gpsimd.memset(eps[:], EPS).then_inc(s_filled, 1)
            L.mark("filled", "eps")
            nc.gpsimd.memset(ones[:], 1.0).then_inc(s_filled, 1)
            L.mark("filled", "ones")
            nc.gpsimd.memset(cst[:].bitcast(F32), 0.0).then_inc(s_filled, 1)
            L.mark("filled", "cst")
            nc.gpsimd.memset(zpad[:], 0.0).then_inc(s_filled, 1)
            L.mark("filled", "zpad")

            pool.wait_ge(s_lf_ready, L.of("lf_ready", "lf"))
            pool.wait_ge(s_mask_in, 64)
            for h in range(HEADS):
                if h >= 2:
                    pool.wait_ge(s_scores, L.of("scores", ("fox", h - 2, 1)))
                for s in range(TB):
                    nc.gpsimd.tensor_scalar(lfw[:, h % 2, s, :], upto[:, s, :], lf[:, 5, s, h:h + 1], None, ALU.mult)\
                        .then_inc(s_lfw, 1)
                    L.mark("lfw", (h, s))

        @block.scalar
        def _(act):
            L = Stream(act, "act", known, traced)
            A = nc.scalar.activation

            def split(elems):
                act.wait_ge(raw_in[L.raw_slot()], L.loads())
                if L.n.get("hi_ready", 0) >= NSPLIT:
                    act.wait_ge(s_chunk_used, L.at("hi_ready", 1 - NSPLIT))
                s, c = L.split_slot(), L.raw_slot()
                A(whi[:, s, 0:elems], raw[:, c, 0:elems], ACT.Copy).then_inc(s_hi_ready, 1)
                L.mark("hi_ready")
                L.add("drained")

            def ahead(group, between=None, later=None, sums=0):
                L.end = L.n.get("hi_ready", 0)
                chunks = group
                for n, elems in enumerate(chunks):
                    if n == 4 and between:
                        between()
                    if n == 6 and later:
                        later()
                    split(elems)
                    L.add("drained", sums)
                if len(chunks) <= 4 and between:
                    between()
                if len(chunks) <= 6 and later:
                    later()

            def done():
                act.wait_ge(s_chunk_used, L.ended())

            def second(nb=4, scale=1.0):
                act.wait_ge(s_half_read, L.at("half_read"))
                A(tmp[:, 0:nb, :], half()[:, 0:nb, T:2 * T], ACT.Copy, scale=scale).then_inc(s_copied, 1)
                L.mark("copied")

            def half():
                return halves[L.n.get("half_read", 0) % 2]

            def turn(k=1):
                L.add("half_read", k)

            def plain(scale=1.0):
                done()
                second(4, scale)
                turn()

            def squares(src, width=4 * T, after=None):
                act.wait_ge(s_half_read, L.at("half_read"))
                for j in range(src.shape[1] // width):
                    n = L.n.get("squared", 0)
                    if after:
                        act.wait_ge(s_stored_x, L.of("stored_x", (after, 4 * j + 3)))
                    if n >= 2:
                        act.wait_ge(s_summed, L.of("summed", ("sq", n - 2)))
                    A(sq[:, n % 2, 0:width], src[:, j * width:(j + 1) * width], ACT.Square).then_inc(s_squared, 1)
                    L.mark("squared", n)

            def root(n, dst, d):
                act.wait_ge(s_summed, L.of("summed", ("sq", L.n["squared"] - 1)))
                A(dst, half()[:, 0, 0:n], ACT.Sqrt, scale=1.0 / d, bias=eps[:]).then_inc(s_root, 1)
                L.mark("root", L.n["squared"])
                turn()

            def round_tiles(name, n, dst, shift=None):
                for k in range(n):
                    act.wait_ge(s_normed, L.of("normed", (name, k)))
                    t = tmp[:, k % 4, :]
                    ins_ = A(dst(k), t, ACT.Copy) if shift is None else A(dst(k), t, ACT.Identity, bias=shift(k))
                    ins_.then_inc(s_rounded, 1)
                    L.mark("rounded", (name, k))
                act.wait_ge(s_act_lo, L.of("act_lo", (name, n - 1)))

            def norm(name, src, dst, shift=None, known=False, after=None):
                if not known:
                    squares(flat(src), after=after)
                    root(T, rstd[:, 0:T], D)
                round_tiles(name, KT, lambda k: dst[:, k, 0:T], shift)

            row_src = {"c": ins["c"][0], "c_ctx": ins["c_ctx"]}
            for name in ("norm_mix_g_2", "norm_mlp_g_2", "norm_final_g_2", "g_final"):
                row_src[name] = ins[name]
            for name in ("b_ada", "g_mix_norm", "g_q_a", "g_kv_a", "g_mix_out", "conv_b", "g_ffn_norm", "ffn_conv_b"):
                row_src[name] = ins[name][0]
            for j in range(3):
                row_src[f"ffn_conv_w{j}"] = ins["ffn_conv_w"][0, j]
            row_src["conv_w"] = ins["conv_w"][0].rearrange("j n -> (j n)")
            for name, (g, r, n) in VEC_AT.items():
                act.dma_start(vrows[r:r + n, g, :], row_src[name].rearrange("(k p) -> k p", p=P)).then_inc(s_vec_in, 16)
            for tb in range(TB):
                act.dma_start(stage[:, 2 + tb, :], ins["ctx"][0, tb * P:(tb + 1) * P, :]).then_inc(s_x_in, 16)
            act.dma_start(bfb[:], ins["b_forget_2"].rearrange("(a n) -> a n", a=1).to_broadcast([P, HEADS]))\
                .then_inc(s_bias_in, 16)
            act.wait_ge(s_columns, L.of("columns", "vec"))
            turn()
            A(silu[:], vec[:, 0, 0:32], ACT.Silu).then_inc(s_silu, 1)
            L.mark("silu", "f32")
            act.wait_ge(s_silu, L.at("silu"))
            act.wait_ge(s_filled, L.of("filled", "cst"))
            A(cst[:, :, 0:2].rearrange("p k a -> p a k"), silu[:].rearrange("p (a k) -> p a k", a=2), ACT.Copy)\
                .then_inc(s_silu, 1)
            L.mark("silu", "hi")
            def early():
                turn(4)
                squares(flat(xt))
                root(T, rstd[:, 0:T], D)
                squares(flat(t16))
                root(T, rstd[:, T:2 * T], D)

            ahead(STD, early)
            with L.loop(3):
                ahead(STD, turn)
                ahead(STD, turn)
            ahead(STD, turn)

            def norm_both():
                turn()
                act.wait_ge(s_columns, L.of("columns", "gain"))
                norm("h1", xt, h1, lambda k: mod_a[:, k, 0:1], True)
                norm("hctx", t16, hctx, lambda k: mod_a[:, k, 1:2], True)

            ahead(KVG, norm_both, None, 1)

            def kv():
                done()
                for _ in range(2):
                    second(3)
                    turn()

            ahead(STD, kv, None, 1)
            ahead(STD, plain, None, 1)
            for n in range(6):
                def conv(n=n):
                    plain()
                    if n % 3 == 1:
                        L.add("padded")
                        act.wait_ge(s_padded, L.at("padded"))
                        for b in range(4):
                            i = 4 * (n // 3) + b
                            A(conv_y[1][:, b, :], zpad[:, b, 1:T + 1], ACT.Identity,
                              scale=col("conv_w", 8 + i), bias=col("conv_b", i)).then_inc(s_tapped, 1)
                            L.mark("tapped", ("c", n, b))

                if n < 5:
                    ahead(STD, conv, None, 1)

            def low_rank():
                squares(flat(qraw))
                root(T, rstd[:, 0:T], QR)
                round_tiles("qn", 4, lambda k: qn[:, k, 0:T])
                squares(flat(kvraw))
                root(2 * T, rstd[:], KVR)
                for k in range(2):
                    act.wait_ge(s_normed, L.of("normed", ("kvn", k)))
                    A(kvn[:, k, :].rearrange("p (s a t) -> p s a t", s=2, a=2)[:, :, 0, :],
                      tmp[:, 2 * k:2 * k + 2, :], ACT.Copy).then_inc(s_rounded, 1)
                    L.mark("rounded", ("kvn", k))
                act.wait_ge(s_act_lo, L.of("act_lo", ("kvn", 1)))

            ahead(QBG, lambda: (conv(5), low_rank()))
            for g in range(4):
                ahead(QBG if g < 3 else KVB, lambda: plain(MLA_SCALE), None, 2 if g == 3 else 0)
            def softmax(tag, h, qb, nk, src, dst, last=False):
                act.wait_ge(s_maxed, L.of("maxed", (tag, h, qb)))
                i = 2 * (h % 2) + qb
                A(dst, src, ACT.Exp, bias=stat[:, i:i + 1], accum_out=stat[:, 8 + i:9 + i]).then_inc(s_expd, 1)
                L.mark("expd", (tag, h, qb))

            def first_attention():
                turn(2)
                L.add("drained", 4 * HEADS)
                for h in range(HEADS + 1):
                    if h < HEADS:
                        for qb in range(TB):
                            softmax("mla", h, qb, 2 * T, bank(2 * (h % 2) + qb), pr1[:, h % 2, qb, :])
                    if h > 0:
                        g = h - 1
                        act.wait_ge(s_pt_turned, L.of("pt_turned", ("mla", g)))
                        A(pt1[:, g % 2, :, :], halves[1][:, 0:2, :].rearrange("p b (s t) -> p (b s) t", s=2),
                          ACT.Copy).then_inc(s_pt_copied, 1)
                        L.mark("pt_copied", ("mla", g))
                turn(2)
                act.wait_ge(s_half_read, L.at("half_read"))
                for j in range(4):
                    squares(flat(t16)[:, j * 4 * T:(j + 1) * 4 * T])
                for j in range(4):
                    act.wait_ge(s_summed, L.of("summed", ("sq", L.n["squared"] - 4 + j)))
                    src_ = halves[(L.n["half_read"] + j // 2) % 2][:, 2 * (j % 2):2 * (j % 2) + 2, :]
                    A(flat(tmp), src_.rearrange("p b n -> p (b n)"), ACT.Sqrt, scale=1.0 / P, bias=eps[:])\
                        .then_inc(s_root, 1)
                    L.mark("root", ("mix", j))
                    act.wait_ge(s_normed, L.of("normed", ("mix", j)))
                    for k in range(4 * j, 4 * j + 4):
                        A(mix[:, k, 0:T], t16[:, k, :], ACT.Copy, scale=col("g_mix_out", k)).then_inc(s_rounded, 1)
                        L.mark("rounded", ("mix", k))
                turn(2)


            for g in range(4):
                def kvb():
                    plain()
                    turn()
                ahead(KVB, kvb, None, 2) if g < 3 else ahead(STD, lambda: (kvb(), first_attention()))

            def taps(name, i, b, out_, tag):
                A(out_, zpad[:, b, 1:T + 1], ACT.Identity, scale=col(name[0], i), bias=col(name[1], i))\
                    .then_inc(s_tapped, 1)
                L.mark("tapped")

            def up(side, tile, nb=4):
                done()
                second(nb)
                turn()
                act.wait_ge(s_half_read, L.at("half_read"))
                for b in range(nb):
                    taps(("ffn_conv_w1", "ffn_conv_b"), tile + (FT * side + b), b, conv_y[side][:, b, :], side)

            def gated(buf, tile, nb=4):
                L.add("conved", 2)
                act.wait_ge(s_conved, L.at("conved"))
                A(conv_y[1][:, 0:nb, :], conv_y[1][:, 0:nb, :], ACT.Silu).then_inc(s_gated, 1)
                L.mark("gated")
                round_batch(hid[buf], tile, nb)

            def round_batch(dst, tile, nb=4):
                L.add("batch")
                act.wait_ge(s_batch, L.at("batch"))
                A(dst[:, bass.ds(tile, nb), 0:T], conv_y[1][:, 0:nb, :], ACT.Copy).then_inc(s_rounded_batch, 1)
                L.mark("rounded_batch")

            for _ in range(3):
                ahead(STD, turn, None, 1)
            ahead(STD, lambda: (turn(), norm("hf", xt, hf, lambda k: mod_f[:, 16 + k:17 + k])))
            with L.loop(2) as i:
                for g in range(2):
                    t = i * 8 + 4 * g
                    ahead(STD, lambda: up(0, t))
                    ahead(STD, lambda: up(1, t), lambda: gated(0, t))
            with L.loop(4) as i:
                ahead(STD, lambda: up(0, i * 4 + HT))
                ahead(STD, lambda: up(1, i * 4 + HT), lambda: gated(1, i * 4))
            with L.loop(2):
                ahead(STD, turn)
                ahead(STD, turn)
            for j in range(3):
                nb = 4 if j < 2 else 3
                nxt = STD if j == 0 else TAIL
                ahead(TAIL if j == 2 else STD, lambda: up(0, 2 * HT + 4 * j, nb))
                ahead(STD if j != 1 else TAIL, lambda: up(1, 2 * HT + 4 * j, nb), lambda: gated(0, 4 * j, nb))
            for g in range(4):
                ahead(STD if g < 3 else DN11, turn)

            def two_norms():
                turn()
                squares(flat(xt))
                root(T, rstd[:, 0:T], D)
                norm("h2", xt, h2, after="g_final")

            for g in range(4):
                ahead(DN11 if g < 3 else STD, turn if g < 3 else two_norms)

            def second_attention(tag, dst):
                for h in range(HEADS + 2):
                    if h > 1:
                        g = h - 2
                        act.wait_ge(s_heads, L.of("heads", (tag, g)))
                        A(dst[:, g, 0:T], bank(6 + g % 2)[:, 0:T], ACT.Copy).then_inc(s_rounded, 1)
                        L.mark("rounded", (tag, g))
                    if h < HEADS:
                        for qb in range(TB):
                            p = p2[:, h % 2, qb, 0:(qb + 1) * P]
                            softmax(tag, h, qb, 0, p, p)
                    if 0 < h <= HEADS:
                        g = h - 1
                        act.wait_ge(s_pt_turned, L.of("pt_turned", (tag, g)))
                        A(pt2[:, g % 2, :, :].rearrange("p a t -> p (a t)")[:, 0:3 * P], bank(4)[:, 0:3 * P], ACT.Copy)\
                            .then_inc(s_pt_copied, 1)
                        L.mark("pt_copied", (tag, g))
                turn(2)

            def gates():
                act.wait_ge(s_half_read, L.at("half_read"))
                A(lf[:, 1], lf[:, 0], ACT.Abs).then_inc(s_act_step, 1)
                L.mark("act_step")
                act.wait_ge(s_act_step, L.at("act_step"))
                A(lf[:, 2], lf[:, 1], ACT.Exp, scale=-1.0).then_inc(s_act_step, 1)
                L.mark("act_step")
                act.wait_ge(s_act_step, L.at("act_step"))
                A(lf[:, 3], lf[:, 2], ACT.Ln, bias=1.0).then_inc(s_gated, 1)
                L.mark("gated", "lf")

            for branch in range(2):
                for g in range(4):
                    ahead(STD, lambda: plain(HEAD_SCALE if g < 2 else 1.0))
                ahead(STD, turn)
                if branch == 0:
                    ahead(STD, lambda: (turn(), second_attention("alibi", heads2[0])))
                else:
                    ahead(FG, turn)
                    ahead(STD, lambda: (turn(), gates(), second_attention("fox", heads2[1])))

            def gate(side, i):
                plain()
                act.wait_ge(s_half_read, L.at("half_read"))
                t = sigs[side][:, bass.ds(i * 4, 4), :]
                A(t, t, ACT.Sigmoid).then_inc(s_gated, 1)
                L.mark("gated")

            with L.loop(3) as i:
                ahead(STD, lambda: gate(0, i))
                ahead(STD, lambda: gate(1, i))
            ahead(STD, lambda: gate(0, 3))
            ahead(PRJ, lambda: gate(1, 3))
            with L.loop(3) as i:
                ahead(PRJ, plain)
                ahead(PRJ, lambda: (plain(), round_batch(h2, i * 4)))
            ahead(PRJ, plain)
            ahead(STD, lambda: (plain(), round_batch(h2, 12)))
            for g in range(4):
                ahead(STD, turn if g < 3 else (lambda: (turn(), norm("hm", xt, hf))))
            for f in range(5):
                if f < 4:
                    with L.loop(2) as i:
                        for g in range(2):
                            ahead(STD, lambda: (plain(), round_batch(hid[f % 2], i * 8 + 4 * g)))
                if 0 < f < 4:
                    with L.loop(2):
                        ahead(STD, turn)
                        ahead(STD, turn)
            for g in range(3):
                ahead(STD, turn)
            turn()
            squares(flat(xt))
            root(T, rstd[:, 0:T], D)

        @block.vector
        def _(dve):
            L = Stream(dve, "dve", known, traced)
            V = nc.vector

            def split(elems):
                s, c = L.split_slot(), L.raw_slot()
                L.add("hi_ready")
                dve.wait_ge(s_hi_ready, L.at("hi_ready"))
                V.tensor_tensor(wlo[:, s, 0:elems], raw[:, c, 0:elems], whi[:, s, 0:elems].bitcast(F32),
                                ALU.subtract).then_inc(s_drained, 1)
                L.mark("drained")

            def sum_chunks(count):
                for _ in range(count):
                    dve.wait_ge(raw_in[L.raw_slot()], L.loads())
                    g, j = divmod(L.n.get("mod_chunks", 0), GC)
                    a = acc[:, g % NACC, :]
                    if j == 0 and g >= NACC:
                        dve.wait_ge(s_mod_summed, g - NACC + 1)
                    if j > 0:
                        dve.wait_ge(s_drained, L.at("drained"))
                    w = raw[:, L.raw_slot(), :].rearrange("p (k n) -> p k n", k=KC)
                    s = silu[:, KC * j:KC * (j + 1)]
                    if j == 0:
                        V.tensor_scalar(a, w[:, 0, :], s[:, 0:1], None, ALU.mult).then_inc(s_dve_step, 1)
                    else:
                        V.scalar_tensor_tensor(a, w[:, 0, :], s[:, 0:1], a, ALU.mult, ALU.add).then_inc(s_dve_step, 1)
                    L.mark("dve_step")
                    dve.wait_ge(s_dve_step, L.at("dve_step"))
                    V.scalar_tensor_tensor(a, w[:, 1, :], s[:, 1:2], a, ALU.mult, ALU.add).then_inc(s_drained, 1)
                    L.mark("drained", ("mod", g) if j == GC - 1 else None)
                    L.add("mod_chunks")

            def ahead(group, between=None, later=None, sums=0):
                L.end = L.n.get("hi_ready", 0)
                chunks = group
                for n, elems in enumerate(chunks):
                    if n == 4 and between:
                        between()
                    if n == 6 and later:
                        later()
                    split(elems)
                    sum_chunks(sums)
                if len(chunks) <= 4 and between:
                    between()
                if len(chunks) <= 6 and later:
                    later()

            def half(ahead_=0):
                return halves[(L.n.get("half_read", 0) + ahead_) % 2]

            def tt(o, a, b, op=ALU.add):
                return V.tensor_tensor(o, a, b, op)

            def copied():
                L.add("copied")
                dve.wait_ge(s_copied, L.at("copied"))

            def halves_sum(dst, nb=4, scale=1.0):
                copied()
                first = half()[:, 0:nb, 0:T]
                if scale == 1.0:
                    tt(dst, first, tmp[:, 0:nb, :]).then_inc(s_half_read, 1)
                    L.mark("half_read")
                else:
                    V.scalar_tensor_tensor(dst, first, scale, tmp[:, 0:nb, :], ALU.mult, ALU.add).then_inc(s_half_read, 1)
                    L.mark("half_read")

            def inverse(n, at=0):
                L.add("norm")
                dve.wait_ge(s_root, L.of("root", L.n["squared"]))
                V.reciprocal(rstd[:, at:at + n], rstd[:, at:at + n]).then_inc(s_half_read, 1)
                L.mark("half_read")
                dve.wait_ge(s_half_read, L.at("half_read"))

            def norm(name, n, src, gain_of, dst, shift=None, at=0):
                def lo(k):
                    dve.wait_ge(s_rounded, L.of("rounded", (name, k)))
                    t, hi = tmp[:, k % 4, :], dst[:, k, 0:T].bitcast(F32)
                    ins_ = tt(dst[:, k, T:2 * T], t, hi, ALU.subtract) if shift is None else \
                        V.scalar_tensor_tensor(dst[:, k, T:2 * T], t, shift(k), hi, ALU.add, ALU.subtract)
                    ins_.then_inc(s_act_lo, 1)
                    L.mark("act_lo", (name, k))

                for k in range(n + 2):
                    if k < n:
                        if k >= 4:
                            dve.wait_ge(s_act_lo, L.at("act_lo", -1))
                        V.scalar_tensor_tensor(tmp[:, k % 4, :], src[:, k, :], gain_of(k), rstd[:, at:at + T],
                                               ALU.mult, ALU.mult).then_inc(s_normed, 1)
                        L.mark("normed", (name, k))
                    if k >= 2:
                        lo(k - 2)

            def square_count(k):
                L.add("squared", k)

            dve.wait_ge(s_turned, L.of("turned", "vec"))
            V.tensor_copy(vec[:, 0, :], half()[:, 0, 0:P]).then_inc(s_columns, 1)
            L.mark("columns", "vec")
            n1, n3 = VEC_ROWS[1], VEC_ROWS[3]
            hv = half()[:, 0:2, :].rearrange("p b (g n) -> p b g n", n=P)
            V.tensor_copy(vec[:, 1:3, 0:n1], hv[:, 0, 1:3, 0:n1]).then_inc(s_columns, 1)
            L.mark("columns")
            V.tensor_copy(vec[:, 3:6, 0:n3], hv[:, 1, 0:3, 0:n3]).then_inc(s_half_read, 1)
            L.mark("half_read")
            dve.wait_ge(s_silu, L.of("silu", "hi"))
            tt(cst[:, :, 2:4].rearrange("p k a -> p a k"), silu[:].rearrange("p (a k) -> p a k", a=2),
               cst[:, :, 0:2].bitcast(F32).rearrange("p k a -> p a k"), ALU.subtract).then_inc(s_cst_ready, 1)
            L.mark("cst_ready", "lo")
            for tb in range(4):
                dve.wait_ge(s_turned, L.of("turned", tb))
                dst = (xt if tb < 2 else t16)[:, :, (tb % 2) * P:(tb % 2 + 1) * P]
                V.tensor_copy(dst, half()[:].rearrange("p b (k t) -> p (b k) t", t=P)).then_inc(s_half_read, 1)
                L.mark("half_read")

            def early():
                square_count(4)
                inverse(T)
                square_count(4)
                inverse(T, T)

            ahead(STD, early)

            def mod_rows():
                dve.wait_ge(s_chunk_used, L.ended())
                s = L.n.get("row_ready", 0) % 2
                V.tensor_copy(row4[:, s, :], half()[0:4, 0, :]).then_inc(s_row_ready, 1)
                L.mark("row_ready")

            def mod_cols(j):
                L.add("row_summed")
                dve.wait_ge(s_row_summed, L.at("row_summed"))
                b = cols("b_ada", j, 4).rearrange("p (a n) -> p n a", a=1).to_broadcast([P, 4, 2])
                tt(mod_a[:, bass.ds(j, 4), :], half()[:, 1, 0:8].rearrange("p (n a) -> p n a", a=2), b)\
                    .then_inc(s_half_read, 1)
                L.mark("half_read")

            with L.loop(3) as i:
                ahead(STD, mod_rows, lambda: mod_cols(i * 8))
                ahead(STD, mod_rows, lambda: mod_cols(i * 8 + 4))
            ahead(STD, mod_rows, lambda: mod_cols(24))

            def norm_both():
                mod_rows()
                mod_cols(28)
                dve.wait_ge(s_half_read, L.at("half_read"))
                for n in range(2):
                    V.scalar_tensor_tensor(gain[:, :, n], mod_a[:, 16:32, n], 1.0, cols("g_mix_norm", 0, 16),
                                           ALU.add, ALU.mult).then_inc(s_columns, 1)
                    L.mark("columns", "gain" if n else None)
                dve.wait_ge(s_columns, L.at("columns"))
                norm("h1", KT, xt, lambda k: gain[:, k, 0:1], h1, lambda k: mod_a[:, k, 0:1])
                dve.wait_ge(s_act_lo, L.at("act_lo"))
                norm("hctx", KT, t16, lambda k: gain[:, k, 1:2], hctx, lambda k: mod_a[:, k, 1:2], T)

            ahead(KVG, norm_both, None, 1)

            def kv():
                for s in range(2):
                    copied()
                    at = slice(s * T, (s + 1) * T)
                    tt(kvraw[:, :, at], half()[:, 0:2, 0:T], tmp[:, 0:2, :]).then_inc(s_dve_step, 1)
                    L.mark("dve_step")
                    tt(krope[ROPE:P, at], half()[ROPE:P, 2, 0:T], tmp[ROPE:P, 2, :]).then_inc(s_half_read, 1)
                    L.mark("half_read")

            def mod(nth=1, b0=0):
                j = 4 * L.n.get("mod_summed", 0)
                L.add("mod_summed")
                dve.wait_ge(s_mod_summed, L.at("mod_summed"))
                tt(mod_f[:, j:j + 4], half(nth)[:, b0, 0:4], cols("b_ada", j + 32, 4)).then_inc(s_mod_read, 1)
                L.mark("mod_read")

            ahead(STD, kv, mod, 1)

            ahead(STD, lambda: halves_sum(qraw[:]), mod, 1)

            def outer_taps(names, i, y, nb=4):
                for b in range(nb):
                    L.add("tapped")
                    dve.wait_ge(s_tapped, L.at("tapped"))
                    V.scalar_tensor_tensor(y[:, b, :], zpad[:, b, 0:T], col(names[0], i + b), y[:, b, :],
                                           ALU.mult, ALU.add).then_inc(s_dve_step, 1)
                    L.mark("dve_step")
                dve.wait_ge(s_dve_step, L.at("dve_step"))
                for b in range(nb):
                    ins_ = V.scalar_tensor_tensor(y[:, b, :], zpad[:, b, 2:T + 2], col(names[1], i + b), y[:, b, :],
                                                  ALU.mult, ALU.add)
                ins_.then_inc(s_conved, 1)
                L.mark("conved")

            dve.wait_ge(s_filled, L.of("filled", "zpad"))
            for n in range(6):
                def conv():
                    if n % 3 == 0:
                        halves_sum(conv_y[0])
                    elif n % 3 == 1:
                        halves_sum(zpad[:, :, 1:T + 1])
                        dve.wait_ge(s_half_read, L.at("half_read"))
                        tt(zpad[:, :, 1:T + 1], zpad[:, :, 1:T + 1], conv_y[0], ALU.mult).then_inc(s_padded, 1)
                        L.mark("padded", (n, 3))
                        i = 4 * (n // 3)
                        dve.wait_ge(s_padded, L.at("padded"))
                        for b in range(4):
                            dve.wait_ge(s_tapped, L.of("tapped", ("c", n, b)))
                            L.add("tapped")
                            V.scalar_tensor_tensor(conv_y[1][:, b, :], zpad[:, b, 0:T], col("conv_w", i + b),
                                                   conv_y[1][:, b, :], ALU.mult, ALU.add).then_inc(s_dve_step, 1)
                            L.mark("dve_step")
                        dve.wait_ge(s_dve_step, L.at("dve_step"))
                        for b in range(4):
                            V.scalar_tensor_tensor(conv_y[1][:, b, :], zpad[:, b, 2:T + 2], col("conv_w", 16 + i + b),
                                                   conv_y[1][:, b, :], ALU.mult, ALU.add).then_inc(s_dve_step, 1)
                            L.mark("dve_step")
                    else:
                        dst = t16[:, 8 + 4 * (n // 3):12 + 4 * (n // 3), :]
                        halves_sum(dst)
                        dve.wait_ge(s_half_read, L.at("half_read"))
                        dve.wait_ge(s_dve_step, L.at("dve_step"))
                        tt(dst, dst, conv_y[1], ALU.mult).then_inc(s_stored_x, 1)
                        L.mark("stored_x", ("conv", n))

                if n < 5:
                    ahead(STD, conv, mod, 1)

            def low_rank():
                square_count(1)
                inverse(T)
                norm("qn", 4, qraw, lambda k: col("g_q_a", k), qn)
                square_count(1)
                inverse(2 * T)
                for k in range(2):
                    V.scalar_tensor_tensor(tmp[:, 2 * k:2 * k + 2, :], kvraw[:, k, :].rearrange("p (s t) -> p s t", s=2),
                                           col("g_kv_a", k), rstd[:].rearrange("p (s t) -> p s t", s=2),
                                           ALU.mult, ALU.mult).then_inc(s_normed, 1)
                    L.mark("normed", ("kvn", k))
                for k in range(2):
                    dve.wait_ge(s_rounded, L.of("rounded", ("kvn", k)))
                    v = kvn[:, k, :].rearrange("p (s a t) -> p s a t", s=2, a=2)
                    tt(v[:, :, 1, :], tmp[:, 2 * k:2 * k + 2, :], v[:, :, 0, :].bitcast(F32), ALU.subtract)\
                        .then_inc(s_act_lo, 1)
                    L.mark("act_lo", ("kvn", k))

            ahead(QBG, lambda: (conv(), low_rank()))
            for g in range(4):
                def qb():
                    copied()
                    V.scalar_tensor_tensor(qt[:, 2 * g:2 * g + 2, :], half()[:, 0:4:2, 0:T], MLA_SCALE,
                                           tmp[:, 0:4:2, :], ALU.mult, ALU.add).then_inc(s_dve_step, 1)
                    L.mark("dve_step")
                    V.scalar_tensor_tensor(qrt[ROPE:P, 2 * g:2 * g + 2, :], half()[ROPE:P, 1:4:2, 0:T], MLA_SCALE,
                                           tmp[ROPE:P, 1:4:2, :], ALU.mult, ALU.add).then_inc(s_half_read, 1)
                    L.mark("half_read", ("q", g))
                ahead(QBG if g < 3 else KVB, qb if g < 3 else (lambda: (qb(), mod(0))), None, 2 if g == 3 else 0)

            def rotate():
                dve.wait_ge(s_rope_in, 32)
                dve.wait_ge(s_projected, L.of("projected", "q"))
                cosine = rope[ROPE:P, 0:1, :].to_broadcast([ROPE, HEADS, T])
                sine = rope[ROPE:P, 1:2, :].to_broadcast([ROPE, HEADS, T])
                s = sq[ROPE:P, :, :].rearrange("p a (h t) -> p (a h) t", t=T)
                tt(qrt[ROPE:P], qrt[ROPE:P], cosine, ALU.mult).then_inc(s_dve_step, 1)
                L.mark("dve_step")
                tt(s, half()[ROPE:P].rearrange("p b (h t) -> p (b h) t", t=T), sine, ALU.mult).then_inc(s_half_read, 1)
                L.mark("half_read")
                dve.wait_ge(s_half_read, L.at("half_read"))
                dve.wait_ge(s_dve_step, L.at("dve_step"))
                tt(qrt[ROPE:P], qrt[ROPE:P], s).then_inc(s_stored_x, 1)
                L.mark("stored_x", "qrt")
                dve.wait_ge(s_stored_x, L.at("stored_x"))
                dve.wait_ge(s_projected, L.of("projected", "k"))
                tt(krope[ROPE:P, 0:T], krope[ROPE:P, 0:T], rope[ROPE:P, 0, :], ALU.mult).then_inc(s_dve_step, 1)
                L.mark("dve_step")
                tt(s[:, 0, :], half()[ROPE:P, 0, 0:T], rope[ROPE:P, 1, :], ALU.mult).then_inc(s_half_read, 1)
                L.mark("half_read")
                dve.wait_ge(s_half_read, L.at("half_read"))
                dve.wait_ge(s_dve_step, L.at("dve_step"))
                tt(krope[ROPE:P, 0:T], krope[ROPE:P, 0:T], s[:, 0, :]).then_inc(s_stored_x, 1)
                L.mark("stored_x", "krope")

            def weigh(tag, g, probs):
                for qb in range(TB):
                    i = 2 * (g % 2) + qb
                    dve.wait_ge(s_expd, L.of("expd", (tag, g, qb)))
                    V.reciprocal(stat[:, 16 + i:17 + i], stat[:, 8 + i:9 + i]).then_inc(s_dve_step, 1)
                    L.mark("dve_step")
                    dve.wait_ge(s_dve_step, L.at("dve_step"))
                    p = probs(qb)
                    V.tensor_scalar(p, p, stat[:, 16 + i:17 + i], None, ALU.mult).then_inc(s_probs, 1)
                    L.mark("probs", (tag, g, qb))

            def first_attention():
                rotate()
                mod(0)
                for h in range(HEADS + 2):
                    if h < HEADS:
                        for qb in range(TB):
                            dve.wait_ge(s_scores, L.of("scores", ("mla", h, qb)))
                            i = 2 * (h % 2) + qb
                            V.tensor_reduce(stat[:, i:i + 1], bank(i), AX, ALU.max, negate=True).then_inc(s_maxed, 1)
                            L.mark("maxed", ("mla", h, qb))
                    if 0 < h <= HEADS:
                        weigh("mla", h - 1, lambda qb: pr1[:, (h - 1) % 2, qb, :])
                        sum_chunks(4)
                    if h > 1:
                        g = h - 2
                        dve.wait_ge(s_heads, L.of("heads", ("mla", g)))
                        ins_ = V.tensor_copy(t16[:, g, :], bank(6 + g % 2)[:, 0:T])
                        ins_.then_inc(s_heads_read, 1)
                        L.mark("heads_read", ("mla", g))
                dve.wait_ge(s_heads_read, L.at("heads_read"))
                V.memset(stat[:, 32:33], 0.0).then_inc(s_half_read, 1)
                L.mark("half_read")
                V.memset(stat[:, 33:34], 0.0).then_inc(s_half_read, 1)
                L.mark("half_read", "mla done")
                for b in range(4):
                    mod(0, b)
                square_count(4)
                for j in range(4):
                    dve.wait_ge(s_root, L.of("root", ("mix", j)))
                    ins_ = V.reciprocal(flat(tmp), flat(tmp))
                    if j % 2 == 0:
                        ins_.then_inc(s_dve_step, 1)
                        L.mark("dve_step")
                        dve.wait_ge(s_dve_step, L.at("dve_step"))
                    else:
                        ins_.then_inc(s_half_read, 1)
                        L.mark("half_read")
                        dve.wait_ge(s_half_read, L.at("half_read"))
                    ks = slice(4 * j, 4 * j + 4)
                    tt(t16[:, ks, :], t16[:, ks, :], tmp[:], ALU.mult).then_inc(s_normed, 1)
                    L.mark("normed", ("mix", j))
                    dve.wait_ge(s_normed, L.at("normed"))
                    for k in range(4 * j, 4 * j + 4):
                        dve.wait_ge(s_rounded, L.of("rounded", ("mix", k)))
                        V.scalar_tensor_tensor(mix[:, k, T:2 * T], t16[:, k, :], col("g_mix_out", k),
                                               mix[:, k, 0:T].bitcast(F32), ALU.mult, ALU.subtract).then_inc(s_act_lo, 1)
                        L.mark("act_lo", ("mix", k))

            for g in range(4):
                def kvb():
                    heads = ktt[:, 2 * g:2 * g + 2, :].rearrange("p h (s t) -> p (h s) t", s=2)
                    halves_sum(heads)
                    dve.wait_ge(s_chunk_used, L.ended())
                    V.tensor_copy(vt[:, :, g * 2 * P:(g + 1) * 2 * P],
                                  half()[:, 0:2, :].rearrange("p b (s n) -> p (b s) n", s=2)).then_inc(s_half_read, 1)
                    L.mark("half_read", ("kv", g))
                ahead(KVB, kvb, None, 2) if g < 3 else ahead(STD, lambda: (kvb(), first_attention()))

            def onto_x(t, gate_of=None):
                if gate_of is mix_gate:
                    dve.wait_ge(s_mod_read, L.at("mod_read"))
                dve.wait_ge(s_chunk_used, L.ended())
                for part in range(2):
                    src = half()[:, :, part * T:(part + 1) * T]
                    if gate_of is None:
                        x4 = xt[:, bass.ds(t, 4), :]
                        ins_ = [tt(x4, src, x4)]
                    else:
                        for b in range(4):
                            xb = xt[:, bass.ds(t + b, 1), :].rearrange("p a t -> p (a t)")
                            one = V.scalar_tensor_tensor(xb, src[:, b, :], gate_of(t + b), xb, ALU.mult, ALU.add)
                            if b < 3:
                                one.then_inc(s_dve_step, 1)
                                L.mark("dve_step")
                        ins_ = [one]
                    if part == 0:
                        ins_[0].then_inc(s_dve_step, 1)
                        L.mark("dve_step")
                        dve.wait_ge(s_dve_step, L.at("dve_step"))
                    else:
                        ins_[0].then_inc(s_half_read, 1)
                        L.mark("half_read")

            def mix_gate(t):
                return mod_f[:, bass.ds(t, 1)]

            def ffn_gate(t):
                return mod_f[:, bass.ds(t + 48, 1)]

            for g in range(3):
                ahead(STD, lambda: onto_x(g * 4, mix_gate), mod if g > 0 else None, 1)

            def ffn_norm():
                onto_x(12, mix_gate)
                mod(0)
                dve.wait_ge(s_mod_read, L.at("mod_read"))
                dve.wait_ge(s_half_read, L.at("half_read"))
                V.scalar_tensor_tensor(gain[:, :, 2], mod_f[:, 32:48], 1.0, cols("g_ffn_norm", 0, 16),
                                       ALU.add, ALU.mult).then_inc(s_columns, 1)
                L.mark("columns", "ffn gain")
                dve.wait_ge(s_columns, L.at("columns"))
                square_count(4)
                inverse(T)
                norm("hf", KT, xt, lambda k: gain[:, k, 2:3], hf, lambda k: mod_f[:, 16 + k:17 + k])

            ahead(STD, ffn_norm)

            def up(side, tile, nb=4):
                copied()
                tt(zpad[:, 0:nb, 1:T + 1], half()[:, 0:nb, 0:T], tmp[:, 0:nb, :]).then_inc(s_half_read, 1)
                L.mark("half_read")
                outer_taps(("ffn_conv_w0", "ffn_conv_w2"), tile + FT * side, conv_y[side], nb)

            def gated(buf, tile, nb=4, key=None):
                L.add("gated")
                dve.wait_ge(s_gated, L.at("gated"))
                dve.wait_ge(s_conved, L.at("conved"))
                y = conv_y[1][:, 0:nb, :]
                tt(y, y, conv_y[0][:, 0:nb, :], ALU.mult).then_inc(s_batch, 1)
                L.mark("batch")
                dve.wait_ge(s_batch, L.at("batch"))
                lo_batch(hid[buf], tile, nb, key)

            def lo_batch(dst, tile, nb=4, key=None):
                L.add("rounded_batch")
                dve.wait_ge(s_rounded_batch, L.at("rounded_batch"))
                tt(dst[:, bass.ds(tile, nb), T:2 * T], conv_y[1][:, 0:nb, :],
                   dst[:, bass.ds(tile, nb), 0:T].bitcast(F32), ALU.subtract).then_inc(s_act_lo, 1)
                L.mark("act_lo", key)

            with L.loop(2) as i:
                for g in range(2):
                    t = i * 8 + 4 * g
                    ahead(STD, lambda: up(0, t))
                    ahead(STD, lambda: up(1, t), lambda: gated(0, t, 4, ("hid", 0) if g else None))
            with L.loop(4) as i:
                ahead(STD, lambda: up(0, i * 4 + HT))
                ahead(STD, lambda: up(1, i * 4 + HT), lambda: gated(1, i * 4, 4, ("hid", 1)))
            with L.loop(2) as i:
                for g in range(2):
                    ahead(STD, lambda: onto_x(i * 8 + 4 * g, ffn_gate))
            for j in range(3):
                nb = 4 if j < 2 else 3
                ahead(TAIL if j == 2 else STD, lambda: up(0, 2 * HT + 4 * j, nb))
                ahead(STD if j != 1 else TAIL, lambda: up(1, 2 * HT + 4 * j, nb),
                      lambda: gated(0, 4 * j, nb, ("hid", 2) if j == 2 else None))
            for g in range(4):
                ahead(STD if g < 3 else DN11, lambda: onto_x(4 * g, ffn_gate))

            def norm_onto_x(name):
                square_count(4)
                inverse(T)
                for k in range(KT):
                    V.scalar_tensor_tensor(xt[:, k, :], xt[:, k, :], col(name, k), rstd[:, 0:T], ALU.mult, ALU.mult)\
                        .then_inc(s_stored_x, 1)
                    L.mark("stored_x", (name, k))

            def norm_h2():
                norm_onto_x("g_final")
                square_count(4)
                dve.wait_ge(s_stored_x, L.at("stored_x"))
                inverse(T)
                norm("h2", KT, xt, lambda k: col("norm_mix_g_2", k), h2)

            for g in range(4):
                ahead(DN11 if g < 3 else STD,
                      lambda: (onto_x(4 * g, ffn_gate), norm_h2() if g == 3 else None))

            def second_attention(tag, dst):
                if tag == "alibi":
                    dve.wait_ge(s_mask_in, 64)
                for h in range(HEADS + 2):
                    if h > 1:
                        g = h - 2
                        dve.wait_ge(s_rounded, L.of("rounded", (tag, g)))
                        tt(dst[:, g, T:2 * T], bank(6 + g % 2)[:, 0:T], dst[:, g, 0:T].bitcast(F32), ALU.subtract)\
                            .then_inc(s_act_lo, 1)
                        L.mark("act_lo", (tag, g))
                    if h < HEADS:
                        for qb in range(TB):
                            dve.wait_ge(s_scores, L.of("scores", (tag, h, qb)))
                            i, nk = 2 * (h % 2) + qb, (qb + 1) * P
                            p = p2[:, h % 2, qb, 0:nk]
                            if tag == "alibi":
                                ins_ = V.scalar_tensor_tensor(p, dist[:, qb, 0:nk], -(2.0 ** -(h + 1)), bank(i)[:, 0:nk],
                                                              ALU.mult, ALU.add)
                            else:
                                ins_ = tt(p, causal[:, qb, 0:nk], bank(i)[:, 0:nk])
                            ins_.then_inc(s_dve_step, 1)
                            L.mark("dve_step")
                            dve.wait_ge(s_dve_step, L.at("dve_step"))
                            V.tensor_reduce(stat[:, i:i + 1], p, AX, ALU.max, negate=True).then_inc(s_maxed, 1)
                            L.mark("maxed", (tag, h, qb))
                    if 0 < h <= HEADS:
                        weigh(tag, h - 1, lambda qb: p2[:, (h - 1) % 2, qb, 0:(qb + 1) * P])
                dve.wait_ge(s_act_lo, L.at("act_lo"))
                V.memset(stat[:, 32:33], 0.0).then_inc(s_half_read, 1)
                L.mark("half_read")
                V.memset(stat[:, 33:34], 0.0).then_inc(s_half_read, 1)
                L.mark("half_read", (tag, "done"))

            def values(g):
                dve.wait_ge(s_chunk_used, L.ended())
                V.tensor_copy(v2[:, :, g * GW:(g + 1) * GW], half()[:, 0:2, :]).then_inc(s_half_read, 1)
                L.mark("half_read")

            def gates():
                dve.wait_ge(s_chunk_used, L.ended())
                dve.wait_ge(s_bias_in, 16)
                b = bfb[:].rearrange("p (a n) -> p a n", a=1).to_broadcast([P, TB, HEADS])
                tt(lf[:, 0], half()[:, 0:2, 0:HEADS], b).then_inc(s_half_read, 1)
                L.mark("half_read")
                dve.wait_ge(s_half_read, L.at("half_read"))
                V.tensor_scalar(lf[:, 4], lf[:, 0], 0.0, None, ALU.min).then_inc(s_dve_step, 1)
                L.mark("dve_step")
                L.add("gated")
                dve.wait_ge(s_gated, L.at("gated"))
                dve.wait_ge(s_dve_step, L.at("dve_step"))
                tt(lf[:, 5], lf[:, 4], lf[:, 3], ALU.subtract).then_inc(s_lf_ready, 1)
                L.mark("lf_ready", "lf")

            for branch in range(2):
                for g in range(4):
                    dst = (q2 if g < 2 else k2)[:, 4 * (g % 2):4 * (g % 2) + 4, :]
                    ahead(STD, lambda: halves_sum(dst, 4, HEAD_SCALE if g < 2 else 1.0))
                ahead(STD, lambda: values(0))
                if branch == 0:
                    ahead(STD, lambda: (values(1), second_attention("alibi", heads2[0])))
                else:
                    ahead(FG, lambda: values(1))
                    ahead(STD, lambda: (gates(), second_attention("fox", heads2[1])))

            def gate(side, i):
                L.add("gated")
                halves_sum(sigs[side][:, bass.ds(i * 4, 4), :])

            with L.loop(3) as i:
                ahead(STD, lambda: gate(0, i))
                ahead(STD, lambda: gate(1, i))
            ahead(STD, lambda: gate(0, 3))
            ahead(PRJ, lambda: gate(1, 3))

            def branch_a(i):
                halves_sum(conv_y[0])
                dve.wait_ge(s_half_read, L.at("half_read"))
                dve.wait_ge(s_gated, L.at("gated"))
                tt(conv_y[0], conv_y[0], sigs[0][:, bass.ds(i * 4, 4), :], ALU.mult).then_inc(s_dve_step, 1)
                L.mark("dve_step")

            def branch_b(i, key=None):
                halves_sum(conv_y[1])
                dve.wait_ge(s_half_read, L.at("half_read"))
                tt(conv_y[1], conv_y[1], sigs[1][:, bass.ds(i * 4, 4), :], ALU.mult).then_inc(s_dve_step, 1)
                L.mark("dve_step")
                dve.wait_ge(s_dve_step, L.at("dve_step"))
                tt(conv_y[1], conv_y[1], conv_y[0]).then_inc(s_batch, 1)
                L.mark("batch")
                dve.wait_ge(s_batch, L.at("batch"))
                lo_batch(h2, i * 4, 4, key)

            with L.loop(3) as i:
                ahead(PRJ, lambda: branch_a(i))
                ahead(PRJ, lambda: branch_b(i))
            ahead(PRJ, lambda: branch_a(3))
            ahead(STD, lambda: branch_b(3, "merged"))

            def norm_hm():
                dve.wait_ge(s_half_read, L.at("half_read"))
                square_count(4)
                inverse(T)
                norm("hm", KT, xt, lambda k: col("norm_mlp_g_2", k), hf)

            for g in range(4):
                ahead(STD, lambda: (onto_x(4 * g), norm_hm() if g == 3 else None))

            def squared_relu(buf, t, key=None):
                halves_sum(conv_y[0])
                dve.wait_ge(s_half_read, L.at("half_read"))
                V.scalar_tensor_tensor(conv_y[1], conv_y[0], 0.0, conv_y[0], ALU.max, ALU.mult).then_inc(s_batch, 1)
                L.mark("batch")
                dve.wait_ge(s_batch, L.at("batch"))
                lo_batch(hid[buf], t, 4, key)

            for f in range(5):
                if f < 4:
                    with L.loop(2) as i:
                        for g in range(2):
                            ahead(STD, lambda: squared_relu(f % 2, i * 8 + 4 * g, ("hid2", f) if g else None))
                if 0 < f < 4:
                    with L.loop(2) as i:
                        for g in range(2):
                            ahead(STD, lambda: onto_x(i * 8 + 4 * g))
            for g in range(3):
                ahead(STD, lambda: onto_x(4 * g))
            L.end = L.n["hi_ready"]
            onto_x(12)
            norm_onto_x("norm_final_g_2")
            for tb in range(TB):
                dve.wait_ge(s_turned, L.of("turned", ("out", tb)))
                V.tensor_copy(outrow[:, tb, :], half()[:].rearrange("p b n -> p (b n)")).then_inc(s_half_read, 1)
                L.mark("half_read", ("row", tb))

        @block.tensor
        def _(pe):
            L = Stream(pe, "pe", known, traced)
            mm = nc.tensor.matmul

            def half(ahead_=0):
                return halves[(L.n.get("half_read", 0) + ahead_) % 2]

            def mods_read():
                if L.mod_open:
                    pe.wait_ge(s_mod_read, L.at("mod_summed"))
                L.mod_open = False

            def free(turns=1):
                if L.n.get("half_read", 0) + turns > 2:
                    pe.wait_ge(s_half_read, L.at("half_read", turns - 2))
                mods_read()

            def mod(nth, b0=0):
                slot = L.n.get("mod_summed", 0) % NACC
                pe.wait_ge(s_drained, L.of("drained", ("mod", L.n.get("mod_summed", 0))))
                for b in range(4):
                    ins_ = mm(half(nth)[:, b0, b:b + 1], acc[:, slot, b * P:(b + 1) * P], ones[:, 0:1], start=True, stop=True)
                ins_.then_inc(s_mod_summed, 1)
                L.mark("mod_summed")
                L.mod_open = True

            def turn(k=1):
                L.add("half_read", k)

            def chunk(width):
                L.add("drained")
                pe.wait_ge(s_drained, L.at("drained"))
                s = L.split_slot()
                return [w[:, s, :] for w in (whi, wlo)]

            def tiles(nk, width, ready=None, sums=0):
                for k0 in range(0, nk, KC):
                    if ready:
                        pe.wait_ge(s_act_lo, L.of("act_lo", (ready, min(k0 + KC, nk) - 1)))
                    hi, lo = chunk(width)
                    L.add("drained", sums)
                    n = min(KC, nk - k0)
                    for k in range(n):
                        at = slice(k * width, (k + 1) * width)
                        yield k0 + k, hi[:, at], lo[:, at], k == n - 1

            def product(operands, nk=KT, width=GW, blocks=(0, P, 2 * P, 3 * P), ready=None, with_mod=False, sums=0):
                free(len(operands))
                for k, hi, lo, last in tiles(nk, width, ready, sums):
                    if with_mod and k == KT // 2:
                        pe.wait_ge(s_half_read, L.at("half_read"))
                        mod(1)
                    for a, (src, nth) in enumerate(operands):
                        for b, at in enumerate(blocks):
                            o = half(nth)[:, b, :]
                            mm(o, hi[:, at:at + P], src(k), start=(k == 0), stop=False)
                            ins_ = mm(o[:, 0:T], lo[:, at:at + P], src(k)[:, 0:T], start=False, stop=(k == nk - 1))
                    if last:
                        ins_.then_inc(s_chunk_used, 1)
                        L.mark("chunk_used")
                        L.add("hi_ready")
                turn(len(operands))

            def of(t, k0=0):
                return [(lambda k: t[:, k0 + k, :], 0)]

            def token_product(t, width=GW, ready=None, nk=KT):
                free()
                for k, hi, lo, last in tiles(nk, width, ready):
                    for tb in range(TB):
                        o = half()[:, tb, 0:width]
                        xh, xl = t[:, k, tb * P:(tb + 1) * P], t[:, k, T + tb * P:T + (tb + 1) * P]
                        mm(o, xh, hi, start=(k == 0), stop=False)
                        mm(o, xh, lo, start=False, stop=False)
                        ins_ = mm(o, xl, hi, start=False, stop=(k == nk - 1))
                    if last:
                        ins_.then_inc(s_chunk_used, 1)
                        L.mark("chunk_used")
                        L.add("hi_ready")
                turn()

            def groups(n, t, k0=0, nk=KT, ready=None):
                with L.loop(n // 2):
                    product(of(t, k0), nk, ready=ready)
                    product(of(t, k0), nk, ready=ready)

            def sums(chunks=4, width=T, n=None):
                free()
                per = 4 * T // width
                for c in range(chunks):
                    j = L.n.get("squared", 0)
                    pe.wait_ge(s_squared, L.of("squared", j))
                    for b in range(per):
                        ins_ = mm(half()[:, 0, 0:width], ones[:], sq[:, j % 2, b * width:(b + 1) * width],
                                  start=(c + b == 0), stop=(c == chunks - 1 and b == per - 1))
                    ins_.then_inc(s_summed, 1)
                    L.mark("summed", ("sq", j))
                    L.add("squared")
                turn()

            pe.wait_ge(s_const_in, 32)
            pe.wait_ge(s_vec_in, 16 * len(VEC_AT))
            for g, n in enumerate(VEC_ROWS):
                ins_ = nc.tensor.transpose(half()[:, g // 3, (g % 3) * P:(g % 3) * P + n], vrows[0:n, g, :], ident[0:n, 0:n])
            ins_.then_inc(s_turned, 1)
            L.mark("turned", "vec")
            turn()
            pe.wait_ge(s_x_in, 64)
            for tb in range(4):
                free()
                for k in range(KT):
                    ins_ = nc.tensor.transpose(half()[:, k // 4, (k % 4) * P:(k % 4 + 1) * P],
                                               stage[:, tb, k * P:(k + 1) * P], ident[:])
                ins_.then_inc(s_turned, 1)
                L.mark("turned", tb)
                turn()
            pe.wait_ge(s_filled, L.of("filled", "ones"))
            sums()
            sums()
            pe.wait_ge(s_cst_ready, L.of("cst_ready", "lo"))

            def turn_rows(nth):
                s = L.n.get("row_ready", 0) % 2
                L.add("row_ready")
                pe.wait_ge(s_row_ready, L.at("row_ready"))
                for b in range(4):
                    ins_ = mm(half(nth)[:, 1, 2 * b:2 * b + 2], row4[0:4, s, b * P:(b + 1) * P], sel[0:4, :], start=True, stop=True)
                ins_.then_inc(s_row_summed, 1)
                L.mark("row_summed")

            def rows(first=False):
                if first:
                    free()
                else:
                    pe.wait_ge(s_half_read, L.at("half_read", -1))
                for k, hi, lo, last in tiles(KT, GW):
                    if k == KT // 2 and not first:
                        turn_rows(1)
                    mm(half()[:, 0, :], cst[:, k, :], hi, start=(k == 0), stop=False)
                    ins_ = mm(half()[:, 0, :], cst[:, k, :], lo, start=False, stop=(k == KT - 1))
                    if last:
                        ins_.then_inc(s_chunk_used, 1)
                        L.mark("chunk_used")
                        L.add("hi_ready")
                turn()

            rows(True)
            with L.loop(3):
                rows()
                rows()
            rows()
            turn_rows(-1)
            product([(lambda k: h1[:, k, :], 0), (lambda k: hctx[:, k, :], 1)], width=KVR + ROPE, blocks=(0, P, KVR + ROPE - P), ready="hctx", sums=1)
            product(of(h1), with_mod=True, sums=1)
            for _ in range(len(CONV_COLS)):
                product(of(h1), with_mod=True, sums=1)
            sums(1)
            sums(1, 2 * T)
            pe.wait_ge(s_act_lo, L.of("act_lo", ("qn", 3)))
            with L.loop(2):
                for _ in range(2):
                    product(of(qn), 4, 384, (0, ROPE, 192, 192 + ROPE))
            free()
            mod(0)
            pe.wait_ge(s_act_lo, L.of("act_lo", ("kvn", 1)))
            for g in range(4):
                free(2)
                for k, hi, lo, last in tiles(KC, GW, sums=2):
                    for b in range(4):
                        o, at, x = half()[:, b, :], (b // 2) * 2 * P, kvn[:, k, (b % 2) * 2 * T:(b % 2 + 1) * 2 * T]
                        mm(o, hi[:, at:at + P], x, start=(k == 0), stop=False)
                        mm(o[:, 0:T], lo[:, at:at + P], x[:, 0:T], start=False, stop=(k == KC - 1))
                parts = [(k, hi2, lo2) for k, hi2, lo2 in
                         [(k, whi[:, L.split_slot(), k * GW:(k + 1) * GW], wlo[:, L.split_slot(), k * GW:(k + 1) * GW]) for k in range(KC)]]
                for s in range(4):
                    o = half(1)[:, s // 2, (s % 2) * 2 * P:(s % 2 + 1) * 2 * P].rearrange("p (h n) -> p h n", h=2)
                    for k, hi, lo in parts:
                        vh, vl = [w.rearrange("p (h a n) -> p h a n", h=2, a=2)[:, :, 1, :] for w in (hi, lo)]
                        base = (s // 2) * 2 * T + (s % 2) * P
                        xh, xl = kvn[:, k, base:base + P], kvn[:, k, base + T:base + T + P]
                        mm(o, xh, vh, start=(k == 0), stop=False)
                        mm(o, xh, vl, start=False, stop=False)
                        ins_ = mm(o, xl, vh, start=False, stop=(k == KC - 1))
                ins_.then_inc(s_chunk_used, 1)
                L.mark("chunk_used")
                L.add("hi_ready")
                turn(2)
            pe.wait_ge(s_rope_in, 32)
            free()
            pe.wait_ge(s_half_read, L.of("half_read", ("q", 3)))
            for b in range(4):
                ins_ = mm(half()[ROPE:P, b, :], swap[ROPE:P, :], qrt[ROPE:P, 2 * b:2 * b + 2, :].rearrange("p h t -> p (h t)"),
                          start=True, stop=True)
            ins_.then_inc(s_projected, 1)
            L.mark("projected", "q")
            turn()
            free()
            mm(half()[ROPE:P, 0, 0:T], swap[ROPE:P, :], krope[ROPE:P, 0:T], start=True, stop=True)\
                .then_inc(s_projected, 1)
            L.mark("projected", "k")
            turn()

            def attention(tag, score, turn_p, weighted):
                free(2)
                for h in range(HEADS + 1):
                    if h < HEADS:
                        for qb in range(TB):
                            score(h, qb, bank(2 * (h % 2) + qb)).then_inc(s_scores, 1)
                            L.mark("scores", (tag, h, qb))
                    if h > 0:
                        g = h - 1
                        for qb in range(TB):
                            pe.wait_ge(s_probs, L.of("probs", (tag, g, qb)))
                            ins_ = turn_p(g, qb)
                        ins_.then_inc(s_pt_turned, 1)
                        L.mark("pt_turned", (tag, g))
                        pe.wait_ge(s_pt_copied, L.of("pt_copied", (tag, g)))
                        if g >= 2 and tag == "mla":
                            pe.wait_ge(s_heads_read, L.of("heads_read", (tag, g - 2)))
                        elif g >= 2:
                            pe.wait_ge(s_act_lo, L.of("act_lo", (tag, g - 2)))
                        weighted(g, bank(6 + g % 2)).then_inc(s_heads, 1)
                        L.mark("heads", (tag, g))
                turn(2)

            def score1(h, qb, o):
                mm(o, qt[:, h, qb * P:(qb + 1) * P], ktt[:, h, :], start=True, stop=False)
                return mm(o, qrt[ROPE:P, h, qb * P:(qb + 1) * P], krope[ROPE:P, :], start=False, stop=True)

            def turn1(h, qb):
                for kb in range(4):
                    at = (kb % 2) * T + qb * P
                    ins_ = nc.tensor.transpose(bank(4 + kb // 2)[:, at:at + P], pr1[:, h % 2, qb, kb * P:(kb + 1) * P], ident[:])
                return ins_

            def weighted1(h, o):
                for kb in range(4):
                    ins_ = mm(o[:, 0:T], vt[:, kb, h * P:(h + 1) * P], pt1[:, h % 2, kb, :], start=(kb == 0), stop=(kb == 3))
                return ins_

            pe.wait_ge(s_stored_x, L.of("stored_x", "krope"))
            free()
            mod(0)
            attention("mla", score1, turn1, weighted1)
            pe.wait_ge(s_half_read, L.of("half_read", "mla done"))
            L.add("drained", 4 * HEADS)
            for b in range(4):
                mod(0, b)
            mods_read()
            for j in range(4):
                n = L.n["squared"]
                pe.wait_ge(s_squared, L.of("squared", n))
                for b in range(2):
                    ins_ = mm(half(j // 2)[:, 2 * (j % 2) + b, :], ones[:], sq[:, n % 2, b * 2 * T:(b + 1) * 2 * T],
                              start=True, stop=True)
                ins_.then_inc(s_summed, 1)
                L.mark("summed", ("sq", n))
                L.add("squared")
            turn(2)
            for g in range(4):
                product(of(mix), ready="mix", with_mod=(g > 1), sums=int(g > 0))
            free()
            mod(0)
            sums()
            with L.loop(2):
                for _ in range(2):
                    product(of(hf), ready="hf")
                    product(of(hf))
            groups(8, hf)
            pe.wait_ge(s_act_lo, L.of("act_lo", ("hid", 0)))
            groups(4, hid[0])
            with L.loop(2):
                product(of(hf))
                product(of(hf))
            product(of(hf), width=3 * P, blocks=(0, P, 2 * P))
            product(of(hf), width=3 * P, blocks=(0, P, 2 * P))
            pe.wait_ge(s_act_lo, L.of("act_lo", ("hid", 1)))
            groups(4, hid[1])
            pe.wait_ge(s_act_lo, L.of("act_lo", ("hid", 2)))
            for g in range(4):
                product(of(hid[0]), FT - 2 * HT)
            sums()
            sums()

            def score2(tag):
                def score(h, qb, o):
                    nk = (qb + 1) * P
                    ins_ = mm(o[:, 0:nk], q2[:, h, qb * P:(qb + 1) * P], k2[:, h, 0:nk], start=True, stop=(tag == "alibi"))
                    if tag == "fox":
                        for s in range(qb + 1):
                            pe.wait_ge(s_lfw, L.of("lfw", (h, s)))
                            ins_ = mm(o[:, 0:nk], lfw[:, h % 2, s, qb * P:(qb + 1) * P], after[:, s, 0:nk], start=False, stop=(s == qb))
                    return ins_
                return score

            def turn2(h, qb):
                for kb in range(qb + 1):
                    at = qb * P if kb == 0 else 2 * P
                    ins_ = nc.tensor.transpose(bank(4)[:, at:at + P], p2[:, h % 2, qb, kb * P:(kb + 1) * P], ident[:])
                return ins_

            def weighted2(h, o):
                pt = pt2[:, h % 2, :, :].rearrange("p a t -> p (a t)")
                mm(o[:, 0:T], v2[:, 0, h * P:(h + 1) * P], pt[:, 0:T], start=True, stop=False)
                return mm(o[:, P:T], v2[:, 1, h * P:(h + 1) * P], pt[:, T:T + P], start=False, stop=True)

            for branch, tag in enumerate(("alibi", "fox")):
                with L.loop(2):
                    for _ in range(2):
                        product(of(h2), ready="h2" if branch == 0 else None)
                token_product(h2)
                token_product(h2)
                if tag == "fox":
                    free()
                    hi, lo = chunk(8)
                    for k in range(KT):
                        at = slice(8 * k, 8 * k + 8)
                        for tb in range(TB):
                            o, xh, xl = half()[:, tb, 0:8], h2[:, k, tb * P:(tb + 1) * P], h2[:, k, T + tb * P:T + (tb + 1) * P]
                            mm(o, xh, hi[:, at], start=(k == 0), stop=False)
                            mm(o, xh, lo[:, at], start=False, stop=False)
                            ins_ = mm(o, xl, hi[:, at], start=False, stop=(k == KT - 1))
                    ins_.then_inc(s_chunk_used, 1)
                    L.mark("chunk_used")
                    L.add("hi_ready")
                    turn()
                    pe.wait_ge(s_mask_in, 64)
                free(2)
                attention(tag, score2(tag), turn2, weighted2)
                pe.wait_ge(s_half_read, L.of("half_read", (tag, "done")))
            with L.loop(4):
                product(of(h2))
                product(of(h2))
            with L.loop(4):
                product(of(heads2[0]), 8)
                product(of(heads2[1]), 8)
            pe.wait_ge(s_act_lo, L.of("act_lo", "merged"))
            groups(4, h2)
            sums()
            for f in range(5):
                if f < 4:
                    groups(4, hf, ready="hm" if f == 0 else None)
                if f > 0:
                    pe.wait_ge(s_act_lo, L.of("act_lo", ("hid2", f - 1)))
                    groups(4, hid[(f - 1) % 2])
            sums()
            for tb in range(TB):
                free()
                for k in range(KT):
                    if tb == 0:
                        pe.wait_ge(s_stored_x, L.of("stored_x", ("norm_final_g_2", k)))
                    ins_ = nc.tensor.transpose(half()[:, k // 4, (k % 4) * P:(k % 4 + 1) * P],
                                               xt[:, k, tb * P:(tb + 1) * P], ident[:])
                ins_.then_inc(s_turned, 1)
                L.mark("turned", ("out", tb))
                turn()


INPUTS = ["x", "c", "ctx", "c_ctx", "w_ada", "b_ada", "g_mix_norm", "w_in", "g_q_a", "w_q_b", "g_kv_a", "w_kv_b",
          "conv_w", "conv_b", "g_mix_out", "w_out", "g_ffn_norm", "w_up", "ffn_conv_w", "ffn_conv_b", "w_down",
          "g_final", "norm_mix_g_2", "w_in_2", "b_forget_2", "w_proj_a_2", "w_proj_b_2", "w_out_2", "norm_mlp_g_2",
          "w_up_2", "w_down_2", "norm_final_g_2"]


def kernel(**inputs):
    import concourse.bacc as bacc
    from concourse.bass_utils import run_bass_kernel_spmd

    arrays = {f"in_{n}": np.ascontiguousarray(inputs[n]) for n in INPUTS}
    tables = {f"table_{n}": a for n, a in constants().items()}

    def trace(known):
        nc = bacc.Bacc("TRN2", target_bir_lowering=False, num_devices=1)
        ins = {n: nc.dram_tensor(f"in_{n}", arrays[f"in_{n}"].shape, F32, kind="ExternalInput").ap() for n in INPUTS}
        consts = {n[6:]: nc.dram_tensor(n, a.shape, F32, kind="ExternalInput").ap() for n, a in tables.items()}
        out = nc.dram_tensor("out", (1, T, D), F32, kind="ExternalOutput").ap()
        traced = {}
        program(nc, ins, consts, out, known, traced)
        return nc, traced

    known = {}
    for _ in range(3):
        nc, traced = trace(known)
        known, before = traced, known
    assert known == before
    r = run_bass_kernel_spmd(nc, [{**arrays, **tables}], core_ids=[0])
    return r.results[0]["out"]
```
